# Optimizing a Trainium2 kernel written in Bass

```python
import math
import jax, jax.numpy as jnp
from jax import lax
import numpy as np

D_MODEL = 2048
BATCH = 1
SEQ = 256
DEPTH = 1

HEAD_DIM = 128
A_HEADS = 12
DILATED_PATTERNS = ((128, 1), (512, 4), (2048, 16))
B_HEADS = 8
M_HEADS = 4
M_HEAD_DIM = 256
MEM_LEN = 256
A_WIDTH = A_HEADS * HEAD_DIM
B_WIDTH = B_HEADS * HEAD_DIM
M_WIDTH = M_HEADS * M_HEAD_DIM
N_BRANCH = 3
BLK = 128
REL_BUCKETS = 32
REL_MAX_DIST = 2048
EPS = 1e-6
IN_WIDTHS = (A_WIDTH, A_WIDTH, A_WIDTH, A_WIDTH,
             B_WIDTH, B_WIDTH, B_WIDTH, B_WIDTH, B_HEADS,
             M_WIDTH, M_WIDTH, N_BRANCH * D_MODEL)
IN_COLS = 4 * A_WIDTH + 4 * B_WIDTH + B_HEADS + 2 * M_WIDTH + N_BRANCH * D_MODEL

kernel_name = "hybrid_gated_dilated_fox_memory_block"

def _rmsnorm(x, g):
    xf = x.astype(jnp.float32)
    y = xf * lax.rsqrt(jnp.mean(xf * xf, axis=-1, keepdims=True) + EPS)
    return (y * g.astype(jnp.float32)).astype(x.dtype)

def _split_cols(a, widths):
    outs, off = [], 0
    for w in widths:
        outs.append(a[..., off:off + w])
        off += w
    return outs

def _rel_bucket(dist):
    max_exact = REL_BUCKETS // 2
    d_f = jnp.maximum(dist, 1).astype(jnp.float32)
    large = max_exact + (jnp.log(d_f / max_exact) / math.log(REL_MAX_DIST / max_exact)
                         * (REL_BUCKETS - max_exact)).astype(jnp.int32)
    large = jnp.minimum(large, REL_BUCKETS - 1)
    return jnp.where(dist < max_exact, dist, large)

def _dilated_pattern(q, k, v, rel_table, window, dil):
    B, S, H, d = q.shape
    L = S // dil
    w_sub = window // dil
    nb = -(-L // BLK)
    Lp = nb * BLK
    N = B * dil

    def to_classes(a):
        return a.reshape(B, L, dil, H, d).transpose(0, 2, 1, 3, 4).reshape(N, L, H, d)

    qs = jnp.pad(to_classes(q), ((0, 0), (0, Lp - L), (0, 0), (0, 0)))
    ks = jnp.pad(to_classes(k), ((0, 0), (BLK, Lp - L), (0, 0), (0, 0)))
    vs = jnp.pad(to_classes(v), ((0, 0), (BLK, Lp - L), (0, 0), (0, 0)))
    qb = qs.reshape(N, nb, BLK, H, d)
    kb = ks.reshape(N, nb + 1, BLK, H, d)
    vb = vs.reshape(N, nb + 1, BLK, H, d)
    kw = jnp.concatenate([kb[:, :-1], kb[:, 1:]], axis=2)
    vw = jnp.concatenate([vb[:, :-1], vb[:, 1:]], axis=2)

    logits = jnp.einsum('nbqhd,nbkhd->nbhqk', qb, kw,
                        preferred_element_type=jnp.float32) * (1.0 / math.sqrt(d))
    delta = jnp.arange(BLK)[:, None] - jnp.arange(2 * BLK)[None, :] + BLK
    key_pos = (jnp.arange(nb) * BLK)[:, None, None] + jnp.arange(2 * BLK)[None, None, :] - BLK
    valid = (delta >= 0)[None] & (delta <= w_sub)[None] & (key_pos >= 0)
    bucket = _rel_bucket(jnp.clip(delta, 0, w_sub) * dil)
    bias = jnp.transpose(rel_table[bucket], (2, 0, 1)).astype(jnp.float32)
    logits = jnp.where(valid[None, :, None], logits + bias[None, None], -jnp.inf)
    mx = jnp.max(logits, axis=-1, keepdims=True)
    p = jnp.exp(logits - mx)
    den = jnp.sum(p, axis=-1)
    o = jnp.einsum('nbhqk,nbkhd->nbqhd', p.astype(v.dtype), vw,
                   preferred_element_type=jnp.float32) / jnp.swapaxes(den, 2, 3)[..., None]
    lse = jnp.swapaxes(mx[..., 0] + jnp.log(den), 2, 3)

    def from_classes(a):
        tail = a.shape[3:]
        a = a.reshape((N, Lp) + tail)[:, :L]
        a = a.reshape((B, dil, L) + tail)
        return jnp.swapaxes(a, 1, 2).reshape((B, S) + tail)

    return from_classes(o), from_classes(lse)

def _dilated_mixture(q, k, v, rel_table):
    outs, lses = [], []
    for window, dil in DILATED_PATTERNS:
        o, lse = _dilated_pattern(q, k, v, rel_table, window, dil)
        outs.append(o)
        lses.append(lse)
    alpha = jax.nn.softmax(jnp.stack(lses, axis=0), axis=0)
    return jnp.einsum('pbsh,pbshd->bshd', alpha, jnp.stack(outs, axis=0))

def _forgetting_attention(q, k, v, log_f):
    B, S, H, d = q.shape
    qt, kt, vt = jnp.swapaxes(q, 1, 2), jnp.swapaxes(k, 1, 2), jnp.swapaxes(v, 1, 2)
    c = jnp.cumsum(jnp.swapaxes(log_f, 1, 2), axis=-1)
    kpos = jnp.arange(S)
    scale = 1.0 / math.sqrt(d)

    def block(n):
        start = n * BLK
        qn = lax.dynamic_slice_in_dim(qt, start, BLK, axis=2)
        cq = lax.dynamic_slice_in_dim(c, start, BLK, axis=2)
        s = jnp.einsum('bhqd,bhkd->bhqk', qn, kt, preferred_element_type=jnp.float32) * scale
        s = s + cq[..., :, None] - c[..., None, :]
        qpos = start + jnp.arange(BLK)
        s = jnp.where(kpos[None, :] <= qpos[:, None], s, -jnp.inf)
        p = jax.nn.softmax(s, axis=-1)
        return jnp.einsum('bhqk,bhkd->bqhd', p.astype(vt.dtype), vt)

    o = lax.map(block, jnp.arange(S // BLK))
    return jnp.swapaxes(o, 0, 1).reshape(B, S, H, d)

def _memory_attention(q, k, v):
    s = jnp.einsum('bshd,bmhd->bhsm', q, k, preferred_element_type=jnp.float32) * (1.0 / math.sqrt(q.shape[-1]))
    p = jax.nn.softmax(s, axis=-1)
    return jnp.einsum('bhsm,bmhd->bshd', p.astype(v.dtype), v)

def setup_inputs(seed: int = 0) -> dict:
    key = jax.random.key(seed)
    ks = jax.random.split(key, 20)
    f32 = jnp.float32

    def gain(k, shape):
        return 1.0 + 0.02 * jax.random.normal(k, shape, f32)

    return {
        "x": jax.random.normal(ks[0], (BATCH, SEQ, D_MODEL), f32),
        "mem": jax.random.normal(ks[1], (BATCH, MEM_LEN, D_MODEL), f32),
        "norm_g": gain(ks[2], (DEPTH, D_MODEL)),
        "mem_norm_g": gain(ks[3], (DEPTH, D_MODEL)),
        "w_in": jax.random.normal(ks[4], (DEPTH, D_MODEL, IN_COLS), f32) * D_MODEL ** -0.5,
        "b_forget": jnp.linspace(2.0, 6.0, B_HEADS, dtype=f32)[None]
                    + 0.1 * jax.random.normal(ks[5], (DEPTH, B_HEADS), f32),
        "b_gate": 0.02 * jax.random.normal(ks[6], (DEPTH, N_BRANCH, D_MODEL), f32),
        "rel_bias": 0.1 * jax.random.normal(ks[7], (REL_BUCKETS, A_HEADS), f32),
        "q_norm_a": gain(ks[8], (DEPTH, HEAD_DIM)),
        "k_norm_a": gain(ks[9], (DEPTH, HEAD_DIM)),
        "q_norm_b": gain(ks[10], (DEPTH, HEAD_DIM)),
        "k_norm_b": gain(ks[11], (DEPTH, HEAD_DIM)),
        "q_norm_m": gain(ks[12], (DEPTH, M_HEAD_DIM)),
        "k_norm_m": gain(ks[13], (DEPTH, M_HEAD_DIM)),
        "w_mem_kv": jax.random.normal(ks[14], (DEPTH, D_MODEL, 2 * M_WIDTH), f32) * D_MODEL ** -0.5,
        "w_proj_a": jax.random.normal(ks[15], (DEPTH, A_WIDTH, D_MODEL), f32) * A_WIDTH ** -0.5,
        "w_proj_b": jax.random.normal(ks[16], (DEPTH, B_WIDTH, D_MODEL), f32) * B_WIDTH ** -0.5,
        "w_proj_m": jax.random.normal(ks[17], (DEPTH, M_WIDTH, D_MODEL), f32) * M_WIDTH ** -0.5,
        "w_out": jax.random.normal(ks[18], (DEPTH, D_MODEL, D_MODEL), f32) * D_MODEL ** -0.5,
    }

def reference(x, mem, norm_g, mem_norm_g, w_in, b_forget, b_gate, rel_bias,
              q_norm_a, k_norm_a, q_norm_b, k_norm_b, q_norm_m, k_norm_m,
              w_mem_kv, w_proj_a, w_proj_b, w_proj_m, w_out):
    B, S, _ = x.shape
    M = mem.shape[1]
    for l in range(DEPTH):
        h = _rmsnorm(x, norm_g[l])
        proj = h @ w_in[l]
        qa, ka, va, za, qb, kb, vb, zb, fb, qm, zm, gl = _split_cols(proj, IN_WIDTHS)

        qa = _rmsnorm(qa.reshape(B, S, A_HEADS, HEAD_DIM), q_norm_a[l])
        ka = _rmsnorm(ka.reshape(B, S, A_HEADS, HEAD_DIM), k_norm_a[l])
        va = va.reshape(B, S, A_HEADS, HEAD_DIM)
        oa = _dilated_mixture(qa, ka, va, rel_bias).reshape(B, S, A_WIDTH).astype(x.dtype)
        ua = (oa * jax.nn.silu(za)) @ w_proj_a[l]

        qb = _rmsnorm(qb.reshape(B, S, B_HEADS, HEAD_DIM), q_norm_b[l])
        kb = _rmsnorm(kb.reshape(B, S, B_HEADS, HEAD_DIM), k_norm_b[l])
        vb = vb.reshape(B, S, B_HEADS, HEAD_DIM)
        log_f = jax.nn.log_sigmoid(fb.astype(jnp.float32) + b_forget[l].astype(jnp.float32))
        ob = _forgetting_attention(qb, kb, vb, log_f).reshape(B, S, B_WIDTH).astype(x.dtype)
        ub = (ob * jax.nn.silu(zb)) @ w_proj_b[l]

        mh = _rmsnorm(mem, mem_norm_g[l])
        km, vm = _split_cols(mh @ w_mem_kv[l], (M_WIDTH, M_WIDTH))
        qm = _rmsnorm(qm.reshape(B, S, M_HEADS, M_HEAD_DIM), q_norm_m[l])
        km = _rmsnorm(km.reshape(B, M, M_HEADS, M_HEAD_DIM), k_norm_m[l])
        vm = vm.reshape(B, M, M_HEADS, M_HEAD_DIM)
        om = _memory_attention(qm, km, vm).reshape(B, S, M_WIDTH).astype(x.dtype)
        um = (om * jax.nn.silu(zm)) @ w_proj_m[l]

        g = jax.nn.sigmoid(gl.reshape(B, S, N_BRANCH, D_MODEL) + b_gate[l])
        merged = g[:, :, 0] * ua + g[:, :, 1] * ub + g[:, :, 2] * um
        x = x + (merged @ w_out[l]).astype(x.dtype)
    return x


_drawn_inputs = setup_inputs


def setup_inputs(seed=0):
    import zlib

    import numpy as np

    out = dict(_drawn_inputs(seed))
    spreads = {}
    factors = {'norm_g': 8.0,
     'mem_norm_g': 8.0,
     'b_gate': 8.0,
     'rel_bias': 8.0,
     'q_norm_a': 8.0,
     'k_norm_a': 8.0,
     'q_norm_b': 8.0,
     'k_norm_b': 8.0,
     'q_norm_m': 8.0,
     'k_norm_m': 8.0}
    for name, (base, spread) in spreads.items():
        noise = np.random.default_rng([zlib.crc32(name.encode()), seed]).standard_normal(out[name].shape)
        drawn = base * np.exp(spread * noise) if base else spread * noise
        out[name] = __import__('jax').numpy.asarray(drawn.astype(out[name].dtype))
    for name, factor in factors.items():
        out[name] = (out[name] * factor).astype(out[name].dtype)
    return out
```

```python
import math

import numpy as np

import concourse.bass as bass
from concourse import mybir
from concourse.alu_op_type import AluOpType as ALU

F32 = mybir.dt.float32
F32R = mybir.dt.float32r
ACT = mybir.ActivationFunctionType
AX = mybir.AxisListType

P = 128
D = 2048
S = 256
TT = S // P
KT = D // P
CW = 512
A_HEADS, B_HEADS, M_HEADS, HD, MD = 12, 8, 4, 128, 256
AW, BW, MW = A_HEADS * HD, B_HEADS * HD, M_HEADS * MD
A0 = 0
B0 = 4 * AW
F0 = B0 + 4 * BW
M0 = F0 + B_HEADS
G0 = M0 + 2 * MW
NCOLS = G0 + 3 * D
EPS = 1e-6
MASKED = 1e30

LK = 4
UK = 2
RING = 4
CU = KT // UK
BODY_U = 4 * CU
PROJ_K = (MW // P, AW // P, BW // P)
MERGE_U = 3 * CU + sum(PROJ_K) // UK
M_GROUPS = MW // CW
A_GROUPS = AW // CW
B_GROUPS = BW // CW
AB_GROUPS = A_GROUPS + B_GROUPS
GROUPS = M_GROUPS + AB_GROUPS
NCH = D // CW
OZ_M, OZ_A, OZ_B = 0, PROJ_K[0], PROJ_K[0] + PROJ_K[1]
SEG = 3 * P

S_SCORES = (0, 1)
S_PROBT = (9, 10)
S_PV = 14
S_QT, S_KT = 15, 23
S_OZT = 20
U_Z = (2, 3)
U_LOGITS = (3, 5)
U_PROBS = (4, 6)
U_COPY = (12, 13)
U_OZ = (17, 18)
U_SQ = (10, 18)
U_NORM = (13, 21)
U_EVAC = (18, 26)
U_SPLIT = (23, 24)
U_V = (27, 28)


def last_use(slot, n):
    return max(x for x in range(n) if x % RING == slot)


def hybrid_block(nc, x, mem, norm_g, mem_norm_g, w_in, b_forget, b_gate, rel_bias,
                 q_norm_a, k_norm_a, q_norm_b, k_norm_b, q_norm_m, k_norm_m,
                 w_mem_kv, w_proj_a, w_proj_b, w_proj_m, w_out, consts, onehot, out):

    def sb(name, shape, dt=F32):
        return nc.alloc_sbuf_tensor(name, shape, dt)

    hT = [sb("hT_hi", [P, KT, S], F32R), sb("hT_lo", [P, KT, S], F32R)]
    mT = [sb("mT_hi", [P, KT, S], F32R), sb("mT_lo", [P, KT, S], F32R)]
    ozT = [sb("ozT_hi", [P, sum(PROJ_K), S], F32R), sb("ozT_lo", [P, sum(PROJ_K), S], F32R)]
    raw = sb("w_raw", [P, RING, LK, CW])
    whi = sb("w_hi", [P, RING, UK, CW], F32R)
    wlo = sb("w_lo", [P, RING, UK, CW], F32R)
    group = sb("group", [P, 8 * 1024])

    def part(at, n):
        return group[:, at:at + n]

    qT = part(0, 1024).rearrange("p (b s) -> p b s", b=4)
    kT = part(1024, 1024).rearrange("p (b s) -> p b s", b=4)
    v_sb = part(2048, 1024).rearrange("p (t c) -> p t c", t=TT)
    silz = part(3072, 1024).rearrange("p (t c) -> p t c", t=TT)
    qn = part(4096, 1024).rearrange("p (t c) -> p t c", t=TT)
    probs = part(5120, 4 * SEG).rearrange("p (h c) -> p h c", h=4)
    probs_m = part(5120, 1024).rearrange("p (h t c) -> p h t c", h=2, t=TT)
    bias = part(5120 + 4 * SEG, 4 * SEG).rearrange("p (h c) -> p h c", h=4)
    g_row = part(0, 2048)
    gm_row = part(2048, 2048)
    mem_sb = part(4096, 4096).rearrange("p (t c) -> p t c", t=TT)
    gates = [part(1024 * i, 1024).rearrange("p (t c) -> p t c", t=TT) for i in range(3)]
    merged, product = silz, qn
    gate_b = part(5120 + 4 * SEG, 3 * CW).rearrange("p (i c) -> p i c", i=3)
    res = [part(0, 1024), part(1024, 1024), part(5120, 1024), part(5120 + 4 * SEG, 1024)]
    res = [r.rearrange("p (t c) -> p t c", t=TT) for r in res]

    cst = sb("cst", [P, P + S + S])
    ident = cst[:, 0:P]
    tri = cst[:, P:P + S]
    causal = cst[:, P + S:P + 2 * S]
    oh = sb("oh", [33, SEG])
    rel = sb("rel", [33, A_HEADS])
    dvec = oh[0:A_HEADS, :]
    gains = sb("gains", [P, 8])
    gq = sb("gq", [P, AB_GROUPS + 2])
    gk = sb("gk", [P, AB_GROUPS + 2])
    gcur = sb("gcur", [P, 2])
    wf = sb("wf", [P, KT, B_HEADS])
    wf_hi, wf_lo = (o[:, 0, 0:KT * B_HEADS].rearrange("p (k h) -> p k h", k=KT) for o in ozT)
    bf = sb("bf", [P, B_HEADS])
    ls = [sb(f"ls{i}", [P, TT, B_HEADS]) for i in range(8)]
    ccol = sb("ccol", [P, TT, B_HEADS])
    half = sb("half", [P, 8])
    ssx = sb("ssx", [P, 4])
    msx = sb("msx", [P, 4])
    rsx = sb("rsx", [P, 4])
    ss = sb("ss", [P, 8])
    ms = sb("ms", [P, 8])
    rs = sb("rs", [P, 8])
    rmin = sb("rmin", [P, 8])
    den = sb("den", [P, 8])
    inv = sb("inv", [P, 8])
    spare = sb("spare", [P, 2])
    rden = sb("rden", [P, 8])

    rel_dram = nc.dram_tensor("rel_by_distance", (A_HEADS, SEG), F32, kind="Internal").ap()
    bias_dram = nc.dram_tensor("bias_tiles", (AB_GROUPS, P, 4, SEG), F32, kind="Internal").ap()

    acc = [[nc.alloc_psum_tensor(f"acc{c}{t}", [P, CW], F32) for t in range(TT)] for c in range(2)]
    side = [nc.alloc_psum_tensor(f"side{i}", [P, CW], F32) for i in range(4)]

    sem = nc.alloc_semaphore
    load_in = [sem(f"load_in{i}") for i in range(RING)]
    x_in = [sem(f"x_in{i}") for i in range(TT)]
    g_in, mem_in, gm_in = sem("g_in"), sem("mem_in"), sem("gm_in")
    cst_in, small_in, wf_in = sem("cst_in"), sem("small_in"), sem("wf_in")
    hi_done, lo_done, unit_used = sem("hi_done"), sem("lo_done"), sem("unit_used")
    chunk_taken = sem("chunk_taken")
    scores_done, logits_done, probs_done = sem("scores_done"), sem("logits_done"), sem("probs_done")
    probT_done, probT_copied, pv_done = sem("probT_done"), sem("probT_copied"), sem("pv_done")
    inv_done, rden_done, oz_done = sem("inv_done"), sem("rden_done"), sem("oz_done")
    ozT_done, oz_hi, oz_lo = sem("ozT_done"), sem("oz_hi"), sem("oz_lo")
    squares, sums, means, roots = sem("squares"), sem("sums"), sem("means"), sem("roots")
    qkT_done, qkT_evac = sem("qkT_done"), sem("qkT_evac")
    z_tanh, gains_set = sem("z_tanh"), sem("gains_set")
    bias_in, bias_out = sem("bias_in"), sem("bias_out")
    gb_in, gate_tanh = sem("gb_in"), sem("gate_tanh")
    mixed, mergedT_done, m_hi, m_lo = sem("mixed"), sem("mergedT_done"), sem("m_hi"), sem("m_lo")
    res_in, out_sem = sem("res_in"), sem("out_sem")
    pre = {n: sem("pre_" + n) for n in (
        "half rel gains sumx meanx rootx xn xT x_hi x_lo wf_hi wf_lo dvec dvec_sb dvec_out "
        "summ meanm rootm mn mTp mT_hi mT_lo "
        "fb v0 v1 vneg e u ln c1 c2 c3 c4 lf wtri ccol ccol_sb crow fbias").split()}

    def at(n, k):
        return n + k

    x_v = x.rearrange("b (t p) d -> (b t) p d", p=P)
    mem_v = mem.rearrange("b (t p) d -> (b t) p d", p=P)
    out_v = out.rearrange("b (t p) d -> (b p) t d", p=P)
    x_c = x.rearrange("b (t p) d -> (b p) t d", p=P)
    w_in_v = w_in.rearrange("l (p k) n -> (l p) k n", k=KT)
    w_kv_v = w_mem_kv.rearrange("l (p k) n -> (l p) k n", k=KT)
    w_pa = w_proj_a.rearrange("l (k p) n -> (l p) k n", p=P)
    w_pb = w_proj_b.rearrange("l (k p) n -> (l p) k n", p=P)
    w_pm = w_proj_m.rearrange("l (k p) n -> (l p) k n", p=P)
    w_o = w_out.rearrange("l (k p) n -> (l p) k n", p=P)

    def body_chunks(kind, b):
        if kind == "m":
            return [(w_in_v[:, :, M0:], b * CW), (w_kv_v, b * CW), (w_kv_v[:, :, MW:], b * CW),
                    (w_in_v[:, :, M0 + MW:], b * CW)]
        if kind == "a":
            return [(w_in_v[:, :, A0 + i * AW:], b * CW) for i in range(4)]
        return [(w_in_v[:, :, B0 + i * BW - A_GROUPS * CW:], b * CW) for i in range(4)]

    block = nc.Block()
    with block as block:

        @block.sync
        def _(sp):
            for t in range(TT):
                sp.dma_start(raw[:, 2 + t].rearrange("p k c -> p (k c)"), x_v[t]).then_inc(x_in[t], 16)
            sp.dma_start(cst[:], consts).then_inc(cst_in, 16)
            sp.dma_start(g_row, norm_g.to_broadcast([P, D])).then_inc(g_in, 16)

            def load(view, col, k, slot):
                sp.dma_start(raw[:, slot], view[:, k:k + LK, bass.ds(col, CW)]).then_inc(load_in[slot], 16)

            def loads(chunks, u0, before):
                i = 0
                for view, col, tiles in chunks:
                    for k in range(0, tiles, LK):
                        slot = i % RING
                        if i >= RING:
                            sp.wait_ge(lo_done, at(u0, 2 * (i - RING) + 2))
                        elif before is not None:
                            sp.wait_ge(lo_done, at(u0, 2 * (last_use(slot, before) - before) + 2))
                        elif slot >= 2:
                            sp.wait_ge(pre["xT"], 8)
                        load(view, col, k, slot)
                        if before is None and i == 1:
                            for t in range(TT):
                                sp.dma_start(mem_sb[:, t], mem_v[t]).then_inc(mem_in, 16)
                            sp.dma_start(gm_row, mem_norm_g.to_broadcast([P, D])).then_inc(gm_in, 16)
                        i += 1

            def body(kind, b, u0, before):
                loads([(w, c, KT) for w, c in body_chunks(kind, b)], u0, before)

            for b in range(M_GROUPS):
                body("m", b, b * BODY_U, None if b == 0 else 2 * CU)
            ab0 = M_GROUPS * BODY_U
            body("a", 0, ab0, 2 * CU)
            with sp.Fori(1, A_GROUPS) as b:
                body("a", b, ab0 + b * BODY_U, 2 * CU)
            with sp.Fori(A_GROUPS, AB_GROUPS) as b:
                body("b", b, ab0 + b * BODY_U, 2 * CU)

            def merge(n, first, u0, before):
                c = (n - first) * CW
                views = [(w_in_v[:, :, G0 + i * D:], KT) for i in (2, 0, 1)]
                views += [(w_pm, PROJ_K[0]), (w_pa, PROJ_K[1]), (w_pb, PROJ_K[2])]
                loads([(w[:, :, first * CW:], c, tiles) for w, tiles in views], u0, before)

            m0 = GROUPS * BODY_U
            merge(0, 0, m0, 2 * CU)
            with sp.Fori(1, NCH) as n:
                merge(n, 1, m0 + n * MERGE_U, MERGE_U // 2)
            loads([(w_o, n * CW, KT) for n in range(NCH)], m0 + NCH * MERGE_U, MERGE_U // 2)

        @block.gpsimd
        def _(pool):
            pool.memset(half[:], -0.5).then_inc(pre["half"], 1)
            pool.wait_ge(pre["half"], 1)
            pool.memset(rel[32:33, :], 1.0).then_inc(pre["rel"], 1)
            pool.wait_ge(pre["rel"], 1)
            for t in range(TT):
                pool.wait_ge(pre["meanx"], t + 1)
                pool.tensor_tensor(rsx[:, t:t + 1], msx[:, t:t + 1], half[:, 0:1], ALU.pow).then_inc(pre["rootx"], 1)
            pool.wait_ge(pre["meanm"], 1)
            pool.tensor_tensor(rsx[:, 2:4], msx[:, 2:4], half[:, 0:2], ALU.pow).then_inc(pre["rootm"], 1)
            for i in range(2 * M_GROUPS):
                pool.wait_ge(means, i + 1)
                pool.tensor_tensor(rs[:, 0:4], ms[:, 0:4], half[:, 0:4], ALU.pow).then_inc(roots, 1)
            with pool.Fori(2 * M_GROUPS, 2 * GROUPS) as i:
                pool.wait_ge(means, i + 1)
                pool.tensor_tensor(rs[:], ms[:], half[:], ALU.pow).then_inc(roots, 1)

        @block.scalar
        def _(act):
            def hi(u0, s, lc, before=BODY_U):
                ld = s // 2
                slot = ld % RING
                act.wait_ge(load_in[slot], at(16 * lc[slot], 16 * (ld // RING + 1)))
                if s >= RING:
                    act.wait_ge(unit_used, at(u0, s - RING + 1))
                elif not (isinstance(u0, int) and u0 == 0):
                    act.wait_ge(unit_used, at(u0, last_use(s, before) - before + 1))
                act.activation(whi[:, s % RING], raw[:, slot, UK * (s % 2):UK * (s % 2) + UK], ACT.Copy)\
                   .then_inc(hi_done, 1)

            with nc.allow_non_contiguous_dma(reason="vectors of a few hundred words, once"):
                for i, (g, w) in enumerate(((q_norm_a, 1), (k_norm_a, 1), (q_norm_b, 1), (k_norm_b, 1),
                                            (q_norm_m, 2), (k_norm_m, 2))):
                    col = i if w == 1 else 4 + 2 * (i - 4)
                    act.dma_start(gains[:, col:col + w], g.rearrange("l (h p) -> p (l h)", p=P))\
                       .then_inc(small_in, 16)
                act.dma_start(wf[:], w_in_v[:, :, F0:F0 + B_HEADS]).then_inc(wf_in, 16)
            act.dma_start(rel[0:32, :], rel_bias).then_inc(small_in, 16)
            act.dma_start(oh[:], onehot).then_inc(small_in, 16)
            act.dma_start(bf[:], b_forget.to_broadcast([P, B_HEADS])).then_inc(small_in, 16)
            for t in range(TT):
                act.wait_ge(x_in[t], 16)
                if t:
                    act.wait_ge(pre["sumx"], 4 * t)
                for j in range(4):
                    act.activation(side[j][:], raw[:, 2 + t, j], ACT.Square, accum_out=ls[t][:, 0, j:j + 1])\
                       .then_inc(pre["sumx"], 1)
            act.wait_ge(pre["dvec"], 1)
            act.activation(dvec, acc[1][1][0:A_HEADS, 0:SEG], ACT.Copy).then_inc(pre["dvec_sb"], 1)
            act.wait_ge(pre["dvec_sb"], 1)
            act.dma_start(rel_dram, dvec).then_inc(pre["dvec_out"], 16)
            act.wait_ge(wf_in, 16)
            act.activation(wf_hi, wf[:], ACT.Copy).then_inc(pre["wf_hi"], 1)
            for j in range(8):
                act.wait_ge(pre["xT"], j + 1)
                bank = (side + acc[0] + acc[1])[j]
                act.activation(hT[0][:, 2 * j:2 * j + 2], bank[:], ACT.Copy).then_inc(pre["x_hi"], 1)
            act.wait_ge(pre["dvec_out"], 16)
            for g in range(A_GROUPS):
                for c0, n, d0 in ((0, 2 * P, 0), (P, P, 2 * P)):
                    src = bass.AP(rel_dram.tensor, g * 4 * SEG + P - 1 + c0, [[SEG, 4], [-1, P], [1, n]])
                    act.dma_start(bias_dram[g, :, :, d0:d0 + n].rearrange("p h c -> h p c"), src).then_inc(bias_out, 16)

            def square(w, c, norm, t):
                act.wait_ge(unit_used, CU * c + CU)
                if isinstance(norm, int) and norm == 0:
                    act.wait_ge(pre["mTp"], 8)
                else:
                    act.wait_ge(qkT_done, at(2 * norm, 0))
                act.activation(qn[:, t], acc[w][t][:], ACT.Square).then_inc(squares, 1)

            def z_post(g, t):
                act.wait_ge(unit_used, BODY_U * g + BODY_U)
                if isinstance(g, int) and g == 0:
                    act.wait_ge(pre["mn"], 2)
                else:
                    act.wait_ge(ozT_done, at(2 * g, 0))
                act.activation(silz[:, t], acc[1][t][:], ACT.Tanh, scale=0.5).then_inc(z_tanh, 1)

            def evac(kind, norm, which, bank, g):
                dst = (qT, kT)[which]
                act.wait_ge(qkT_done, at(2 * norm, bank + 1))
                if not (isinstance(g, int) and g == 0):
                    act.wait_ge(scores_done, at(2 * g, 0))
                else:
                    act.wait_ge(pre["xn"], 2)
                act.wait_ge(pre["gains"], 1)
                ps = side[2 + bank]
                if kind == "m":
                    for i in range(2):
                        o = act.activation(dst[:, 2 * bank + i], ps[:, i * S:(i + 1) * S], ACT.Copy,
                                           scale=(gq, gk)[which][:, AB_GROUPS + i:AB_GROUPS + i + 1])
                else:
                    act.wait_ge(gains_set, at(g, 1 - M_GROUPS))
                    o = act.activation(dst[:, 2 * bank:2 * bank + 2], ps[:], ACT.Copy,
                                       scale=gcur[:, which:which + 1])
                o.then_inc(qkT_evac, 1)

            def exps(kind, a, step):
                act.wait_ge(logits_done, at(2 * a, step + 1))
                if kind == "m":
                    if a > 0:
                        act.wait_ge(pv_done, 2 * a)
                    for t in range(TT):
                        i = 2 * step + t
                        o = act.activation(probs_m[:, step, t], side[step][:, t * S:(t + 1) * S], ACT.Exp,
                                           bias=rmin[:, i:i + 1], scale=-1.0, accum_out=den[:, i:i + 1])
                else:
                    for h in (2 * step, 2 * step + 1):
                        for i, c0, n in ((2 * h, 0, 2 * P), (2 * h + 1, 2 * P, P)):
                            o = act.activation(probs[:, h, c0:c0 + n], probs[:, h, c0:c0 + n], ACT.Exp,
                                               bias=rmin[:, i:i + 1], scale=-1.0, accum_out=den[:, i:i + 1])
                o.then_inc(probs_done, 1)

            def split_oz(k0, a, bank):
                act.wait_ge(ozT_done, at(2 * a, bank + 1))
                act.wait_ge(pre["fb"], 1)
                act.activation(ozT[0][:, bass.ds(k0 + 2 * bank, 2)], side[bank][:], ACT.Copy).then_inc(oz_hi, 1)

            def attention(kind, a, k0, s):
                if s in U_PROBS:
                    exps(kind, a, U_PROBS.index(s))
                if s in U_SPLIT:
                    split_oz(k0, a, U_SPLIT.index(s))

            def body(kind, g, b, lc, attn):
                u0 = g * BODY_U
                for s in range(BODY_U):
                    hi(u0, s, lc)
                    if attn is not None:
                        if s in U_Z:
                            z_post(attn[1], U_Z.index(s))
                        attention(*attn, s)
                    for w in range(2):
                        for t in range(TT):
                            if s == U_SQ[w] + t:
                                square(w, 4 * g + w, 2 * g + w, t)
                            if s == U_EVAC[w] + t:
                                evac(kind, 2 * g + w, w, t, g)
                    if attn is not None and kind == "ab" and s == 11:
                        if not (isinstance(b, int) and b == 0):
                            act.wait_ge(logits_done, at(2 * g, 0))
                            act.dma_start(bias, bias_dram[bass.ds(b, 1)].rearrange("g p h c -> (g p) h c"))\
                               .then_inc(bias_in, 16)
                        else:
                            act.wait_ge(bias_out, 16 * (2 * A_GROUPS + B_GROUPS))
                            act.dma_start(bias, bias_dram[0]).then_inc(bias_in, 16)
                    if attn is None:
                        if s < TT:
                            act.wait_ge(mem_in, 16 * TT)
                            act.wait_ge(pre["x_lo"], 4)
                            if s:
                                act.wait_ge(pre["summ"], 4 * s)
                            for j in range(4):
                                act.activation(side[j][:], mem_sb[:, s, CW * j:CW * (j + 1)], ACT.Square,
                                               accum_out=ls[2 + s][:, 0, j:j + 1]).then_inc(pre["summ"], 1)
                        for r in range(2):
                            for j in range(4):
                                if s == 5 + 3 * r + j // 2:
                                    act.wait_ge(pre["mTp"], 4 * r + j + 1)
                                    act.activation(mT[0][:, 8 * r + 2 * j:8 * r + 2 * j + 2], side[j][:],
                                                   ACT.Copy).then_inc(pre["mT_hi"], 1)
                        if s == 12:
                            act.wait_ge(pre["vneg"], 1)
                            act.activation(ls[3][:], ls[2][:], ACT.Exp).then_inc(pre["e"], 1)
                        if s == 14:
                            act.wait_ge(pre["u"], 1)
                            act.activation(ls[5][:], ls[4][:], ACT.Ln).then_inc(pre["ln"], 1)
                        if s in (24, 29):
                            i = (24, 29).index(s)
                            act.wait_ge(pre["fbias"], i + 1)
                            act.dma_start(bias_dram[A_GROUPS + i], bias).then_inc(bias_out, 16)

            per = 2 * CU // RING
            body("m", 0, 0, [0] * 4, None)
            body("m", 1, 1, [per] * 4, ("m", 0, OZ_M))
            body("ab", 2, 0, [2 * per] * 4, ("m", 1, OZ_M + 4))
            with act.Fori(1, AB_GROUPS) as b:
                body("ab", b + M_GROUPS, b, [(b + M_GROUPS) * per] * 4,
                     ("ab", b + M_GROUPS - 1, OZ_A + 4 * (b - 1)))

            m0 = GROUPS * BODY_U
            base = [GROUPS * per] * 4
            merge_l = [len(range(s, MERGE_U // 2, RING)) for s in range(RING)]

            def merged_split(n, bank):
                act.wait_ge(mergedT_done, at(2 * n, bank + 1))
                act.wait_ge(unit_used, M_GROUPS * BODY_U)
                act.activation(mT[0][:, bass.ds(4 * n + 2 * bank, 2)], side[bank][:], ACT.Copy).then_inc(m_hi, 1)

            def merge(n, attn):
                lc = [base[s] + n * merge_l[s] for s in range(RING)]
                for s in range(MERGE_U):
                    hi(m0 + n * MERGE_U, s, lc, BODY_U if attn else MERGE_U)
                    if attn:
                        if s in U_Z:
                            z_post(attn[1], U_Z.index(s))
                        attention(*attn, s)
                    elif s in (8, 9):
                        merged_split(n - 1, s - 8)
                    if s == 7:
                        if attn:
                            act.wait_ge(logits_done, 2 * GROUPS)
                            for i, src in enumerate((2, 0, 1)):
                                act.dma_start(gate_b[:, i], b_gate[0, src:src + 1, 0:CW].to_broadcast([P, CW]))\
                                   .then_inc(gb_in, 16)
                        else:
                            act.wait_ge(chunk_taken, 2 * (4 * GROUPS + 6 * n))
                            for i, src in enumerate((2, 0, 1)):
                                act.dma_start(gate_b[:, i], b_gate[0, src:src + 1, bass.ds(n * CW, CW)]
                                              .to_broadcast([P, CW])).then_inc(gb_in, 16)
                    for i in range(3):
                        for t in range(TT):
                            if s == 8 * i + 11 + t:
                                act.wait_ge(chunk_taken, at(2 * (4 * GROUPS + 6 * n), 2 * i + t + 1))
                                act.activation(gates[i][:, t], gates[i][:, t], ACT.Tanh, scale=0.5)\
                                   .then_inc(gate_tanh, 1)

            merge(0, ("ab", GROUPS - 1, OZ_A + 4 * (AB_GROUPS - 1)))
            with act.Fori(1, NCH) as n:
                merge(n, None)

            lc = [base[s] + NCH * merge_l[s] for s in range(RING)]
            u0 = m0 + NCH * MERGE_U
            act.wait_ge(chunk_taken, 2 * (4 * GROUPS + 6 * NCH - 1))
            for n in range(NCH):
                act.dma_start(res[n], x_c[:, :, n * CW:(n + 1) * CW]).then_inc(res_in, 16)
            for s in range(NCH * CU):
                hi(u0, s, lc, MERGE_U)
                if s in (4, 5):
                    merged_split(NCH - 1, s - 4)
                if s >= CU and s % CU == 5:
                    n = s // CU - 1
                    act.wait_ge(chunk_taken, 2 * (4 * GROUPS + 6 * NCH + n + 1))
                    act.dma_start(out_v[:, :, n * CW:(n + 1) * CW], res[n]).then_inc(out_sem, 16)
            for t in range(TT):
                act.wait_ge(chunk_taken, 2 * (4 * GROUPS + 6 * NCH + NCH - 1) + t + 1)
                act.dma_start(out_v[:, t, (NCH - 1) * CW:], res[NCH - 1][:, t]).then_inc(out_sem, 16)
            act.wait_ge(out_sem, 16 * (NCH + 1))

        @block.vector
        def _(dve):
            def lo(u0, s):
                dve.wait_ge(hi_done, at(u0, s + 1))
                dve.tensor_tensor(wlo[:, s % RING], raw[:, (s // 2) % RING, UK * (s % 2):UK * (s % 2) + UK],
                                  whi[:, s % RING].bitcast(F32), ALU.subtract).then_inc(lo_done, 1)

            def chain(name, n, ins):
                ins.then_inc(pre[name], 1)
                dve.wait_ge(pre[name], n)

            for t in range(TT):
                dve.wait_ge(pre["sumx"], 4 * (t + 1))
                chain("c1", t + 1, dve.reduce_sum(ssx[:, t:t + 1], ls[t][:, 0, 0:4], AX.X))
                dve.tensor_scalar(msx[:, t:t + 1], ssx[:, t:t + 1], 1.0 / D, EPS, ALU.mult, ALU.add)\
                   .then_inc(pre["meanx"], 1)
            dve.wait_ge(g_in, 16)
            for t in range(TT):
                dve.wait_ge(pre["rootx"], t + 1)
                xr = raw[:, 2 + t].rearrange("p k c -> p (k c)")
                dve.scalar_tensor_tensor(xr, xr, rsx[:, t:t + 1], g_row, ALU.mult, ALU.mult).then_inc(pre["xn"], 1)
            dve.wait_ge(pre["wf_hi"], 1)
            dve.tensor_tensor(wf_lo, wf[:], wf_hi.bitcast(F32), ALU.subtract).then_inc(pre["wf_lo"], 1)
            dve.wait_ge(small_in, 16 * 9)
            for i in range(AB_GROUPS):
                c = 0 if i < A_GROUPS else 2
                dve.tensor_scalar(gq[:, i:i + 1], gains[:, c:c + 1], -HD ** -0.5, None, ALU.mult)
                dve.tensor_copy(gk[:, i:i + 1], gains[:, c + 1:c + 2])
            dve.tensor_scalar(gq[:, AB_GROUPS:], gains[:, 4:6], -MD ** -0.5, None, ALU.mult)
            dve.tensor_copy(gk[:, AB_GROUPS:], gains[:, 6:8]).then_inc(pre["gains"], 1)
            for j in range(8):
                dve.wait_ge(pre["x_hi"], j + 1)
                bank = (side + acc[0] + acc[1])[j]
                dve.tensor_tensor(hT[1][:, 2 * j:2 * j + 2], bank[:].rearrange("p (k s) -> p k s", k=2),
                                  hT[0][:, 2 * j:2 * j + 2].bitcast(F32), ALU.subtract).then_inc(pre["x_lo"], 1)

            def norm_sums(g, norm, kind):
                heads, dim = (4, HD) if kind == "ab" else (2, MD)
                dve.wait_ge(squares, at(2 * norm, 2))
                dve.reduce_sum(ss[:, 0:2 * heads], qn.rearrange("p t (h d) -> p (t h) d", d=dim), AX.X)\
                   .then_inc(sums, 1)
                dve.wait_ge(sums, at(norm, 1))
                dve.tensor_scalar(ms[:, 0:2 * heads], ss[:, 0:2 * heads], 1.0 / dim, EPS, ALU.mult, ALU.add)\
                   .then_inc(means, 1)

            def normalise(kind, norm, w, t):
                heads, dim = (4, HD) if kind == "ab" else (2, MD)
                dve.wait_ge(roots, at(norm, 1))
                r = rs[:, t * heads:(t + 1) * heads].rearrange("p (h o) -> p h o", o=1).to_broadcast([P, heads, dim])
                dve.tensor_tensor(qn[:, t].rearrange("p (h d) -> p h d", d=dim),
                                  acc[w][t][:].rearrange("p (h d) -> p h d", d=dim), r, ALU.mult)\
                   .then_inc(chunk_taken, 1)

            def silu(g, t):
                dve.wait_ge(z_tanh, at(2 * g, t + 1))
                dve.scalar_tensor_tensor(silz[:, t], silz[:, t], 1.0, acc[1][t][:], ALU.add, ALU.mult)\
                   .then_inc(chunk_taken, 1)

            def logits(kind, a, step):
                dve.wait_ge(scores_done, at(2 * a, step + 1))
                if kind == "m":
                    dve.tensor_reduce(rmin[:, 2 * step:2 * step + 2], side[step][:].rearrange("p (t c) -> p t c", t=TT),
                                      AX.X, ALU.min).then_inc(logits_done, 1)
                    return
                dve.wait_ge(bias_in, at(16 * (a - M_GROUPS), 16))
                dve.wait_ge(pv_done, at(2 * a, 0))
                dve.wait_ge(pre["crow"], 2)
                dve.memset(spare[:, step:step + 1], 0.0)
                for h in (2 * step, 2 * step + 1):
                    for i, c0, n in ((2 * h, 0, 2 * P), (2 * h + 1, 2 * P, P)):
                        o = dve.tensor_tensor_reduce(out=probs[:, h, c0:c0 + n], in0=side[h][:, c0:c0 + n],
                                                     in1=bias[:, h, c0:c0 + n], scale=1.0, scalar=3e38,
                                                     op0=ALU.add, op1=ALU.min, accum_out=rmin[:, i:i + 1])
                o.then_inc(logits_done, 1)

            def copy_probT(kind, a, step):
                dve.wait_ge(probT_done, at(2 * a, step + 1))
                if kind == "m":
                    o = dve.tensor_copy(probs_m[:, step].rearrange("p t c -> p (t c)"), side[step][:])
                else:
                    for h in (2 * step, 2 * step + 1):
                        o = dve.tensor_copy(probs[:, h], side[h][:, 0:SEG])
                o.then_inc(probT_copied, 1)

            def half_inverse(kind, a):
                n = 8 if kind == "ab" else 4
                dve.wait_ge(probs_done, at(2 * a, 2))
                dve.reciprocal(inv[:, 0:n], den[:, 0:n]).then_inc(inv_done, 1)
                dve.wait_ge(inv_done, at(a, 1))
                dve.tensor_scalar(rden[:, 0:n], inv[:, 0:n], 0.5, None, ALU.mult).then_inc(rden_done, 1)

            def gate_output(kind, a, step):
                dve.wait_ge(pv_done, at(2 * a, step + 1))
                dve.wait_ge(rden_done, at(a, 1))
                dve.wait_ge(chunk_taken, at(8 * a, 8))
                for j in range(2):
                    for t in range(TT):
                        if kind == "m":
                            if j:
                                continue
                            i, c0, n, ps = 2 * step + t, step * MD, MD, side[step][:, t * MD:(t + 1) * MD]
                        else:
                            h = 2 * step + j
                            i, c0, n = 2 * h + 1 - t, h * HD, HD
                            ps = side[step][:, j * S + t * P:j * S + (t + 1) * P]
                        o = dve.scalar_tensor_tensor(silz[:, t, c0:c0 + n], ps, rden[:, i:i + 1],
                                                     silz[:, t, c0:c0 + n], ALU.mult, ALU.mult)
                o.then_inc(oz_done, 1)

            def split_oz(k0, a, bank):
                dve.wait_ge(oz_hi, at(2 * a, bank + 1))
                dve.tensor_tensor(ozT[1][:, bass.ds(k0 + 2 * bank, 2)], side[bank][:].rearrange("p (k s) -> p k s", k=2),
                                  ozT[0][:, bass.ds(k0 + 2 * bank, 2)].bitcast(F32), ALU.subtract).then_inc(oz_lo, 1)

            def attention(kind, a, k0, s):
                if s in U_LOGITS:
                    logits(kind, a, U_LOGITS.index(s))
                if s in U_COPY:
                    copy_probT(kind, a, U_COPY.index(s))
                if s == U_COPY[1] + 1:
                    half_inverse(kind, a)
                if s in U_OZ:
                    gate_output(kind, a, U_OZ.index(s))
                if s in U_SPLIT:
                    split_oz(k0, a, U_SPLIT.index(s))

            def forget_bias(i):
                for h in range(4):
                    hh = 4 * i + h
                    ps = side[h // 2]
                    c0 = (h % 2) * S
                    dve.scalar_tensor_tensor(bias[:, h, 0:2 * P], ps[:, c0:c0 + 2 * P], ccol[:, 1, hh:hh + 1],
                                             causal[:, 0:2 * P], ALU.subtract, ALU.add)
                    o = dve.scalar_tensor_tensor(bias[:, h, 2 * P:], ps[:, c0:c0 + P], ccol[:, 0, hh:hh + 1],
                                                 causal[:, P:], ALU.subtract, ALU.add)
                o.then_inc(pre["fbias"], 1)

            def forget_rows(i):
                for h in range(4):
                    hh = 4 * i + h
                    dve.tensor_scalar(probs[:, h, 0:2 * P], tri, ls[7][:, 0, hh:hh + 1], None, ALU.mult)
                    o = dve.tensor_scalar(probs[:, h, 2 * P:], tri[:, 0:P], ls[7][:, 1, hh:hh + 1], None, ALU.mult)
                o.then_inc(pre["wtri"], 1)

            def beside_first(s):
                if s == 2:
                    dve.wait_ge(pre["summ"], 8)
                    for t in range(TT):
                        o = dve.reduce_sum(ssx[:, 2 + t:3 + t], ls[2 + t][:, 0, 0:4], AX.X)
                    chain("c1", 3, o)
                    dve.tensor_scalar(msx[:, 2:4], ssx[:, 2:4], 1.0 / D, EPS, ALU.mult, ALU.add)\
                       .then_inc(pre["meanm"], 1)
                if s in (3, 4):
                    t = s - 3
                    dve.wait_ge(gm_in, 16)
                    dve.wait_ge(pre["rootm"], 1)
                    dve.scalar_tensor_tensor(mem_sb[:, t], mem_sb[:, t], rsx[:, 2 + t:3 + t], gm_row,
                                             ALU.mult, ALU.mult).then_inc(pre["mn"], 1)
                for r in range(2):
                    for j in range(4):
                        if s == 5 + 3 * r + j // 2:
                            dve.wait_ge(pre["mT_hi"], 4 * r + j + 1)
                            dve.tensor_tensor(mT[1][:, 8 * r + 2 * j:8 * r + 2 * j + 2],
                                              side[j][:].rearrange("p (k s) -> p k s", k=2),
                                              mT[0][:, 8 * r + 2 * j:8 * r + 2 * j + 2].bitcast(F32),
                                              ALU.subtract).then_inc(pre["mT_lo"], 1)
                if s == 11:
                    dve.wait_ge(pre["fb"], 1)
                    for t in range(TT):
                        o = dve.tensor_tensor(ls[0][:, t], side[0][:, t * B_HEADS:(t + 1) * B_HEADS], bf[:], ALU.add)
                    chain("v0", 1, o)
                    chain("v1", 1, dve.tensor_scalar(ls[1][:], ls[0][:], -1.0, None, ALU.mult))
                    dve.tensor_tensor(ls[2][:], ls[0][:], ls[1][:], ALU.min).then_inc(pre["vneg"], 1)
                if s == 13:
                    dve.wait_ge(pre["e"], 1)
                    dve.tensor_scalar(ls[4][:], ls[3][:], 1.0, None, ALU.add).then_inc(pre["u"], 1)
                if s == 15:
                    dve.wait_ge(pre["ln"], 1)
                    chain("c2", 1, dve.tensor_scalar(ls[1][:], ls[4][:], -1.0, None, ALU.add))
                    chain("c2", 2, dve.tensor_tensor(ls[2][:], ls[3][:], ls[1][:], ALU.subtract))
                    chain("c2", 3, dve.reciprocal(ls[6][:], ls[4][:]))
                    chain("c2", 4, dve.tensor_tensor(ls[1][:], ls[2][:], ls[6][:], ALU.mult))
                    chain("c2", 5, dve.tensor_tensor(ls[2][:], ls[1][:], ls[5][:], ALU.add))
                    chain("c2", 6, dve.tensor_scalar(ls[6][:], ls[0][:], 0.0, None, ALU.min))
                    chain("c2", 7, dve.tensor_tensor(ls[7][:], ls[6][:], ls[2][:], ALU.subtract))
                    dve.tensor_copy(ls[3][:], ls[7][:]).then_inc(pre["lf"], 1)
                if s == 16:
                    forget_rows(0)
                if s == 19:
                    dve.wait_ge(pre["ccol"], 1)
                    dve.tensor_copy(ccol[:].rearrange("p t h -> p (t h)"), side[0][:, 0:TT * B_HEADS])\
                       .then_inc(pre["ccol_sb"], 1)
                if s == 23:
                    dve.wait_ge(pre["crow"], 1)
                    dve.wait_ge(pre["ccol_sb"], 1)
                    forget_bias(0)
                if s == 24:
                    forget_rows(1)
                if s == 28:
                    dve.wait_ge(pre["crow"], 2)
                    dve.wait_ge(bias_out, 16 * (2 * A_GROUPS + 1))
                    forget_bias(1)

            def body(kind, g, attn, b=None):
                u0 = g * BODY_U
                for s in range(BODY_U):
                    lo(u0, s)
                    if s == 9 and kind == "ab":
                        dve.wait_ge(qkT_evac, at(4 * g, 0))
                        dve.wait_ge(pre["gains"], 1)
                        dve.tensor_copy(gcur[:, 0:1], gq[:, bass.ds(b, 1)])
                        dve.tensor_copy(gcur[:, 1:2], gk[:, bass.ds(b, 1)]).then_inc(gains_set, 1)
                    if attn is None:
                        beside_first(s)
                    else:
                        for t in range(TT):
                            if s == U_Z[t] + 1:
                                silu(attn[1], t)
                        attention(*attn, s)
                    for w in range(2):
                        if s == U_SQ[w] + 1:
                            norm_sums(g, 2 * g + w, kind)
                        for t in range(TT):
                            if s == U_NORM[w] + t:
                                normalise(kind, 2 * g + w, w, t)
                    if s in U_V:
                        t = U_V.index(s)
                        dve.wait_ge(unit_used, at(u0, 3 * CU))
                        if attn is not None:
                            dve.wait_ge(pv_done, at(2 * g, 0))
                        dve.tensor_copy(v_sb[:, t], acc[0][t][:]).then_inc(chunk_taken, 1)

            body("m", 0, None)
            body("m", 1, ("m", 0, OZ_M))
            body("ab", 2, ("m", 1, OZ_M + 4), 0)
            with dve.Fori(1, AB_GROUPS) as b:
                body("ab", b + M_GROUPS, ("ab", b + M_GROUPS - 1, OZ_A + 4 * (b - 1)), b)

            m0 = GROUPS * BODY_U
            c0 = 4 * GROUPS

            def mix_last(n, t, c):
                dve.wait_ge(unit_used, m0 + n * MERGE_U + MERGE_U)
                dve.wait_ge(gate_tanh, at(6 * n, 6))
                dve.wait_ge(mixed, at(4 * n, 2))
                dve.scalar_tensor_tensor(product[:, t], gates[2][:, t], 1.0, acc[1][t][:], ALU.add, ALU.mult)\
                   .then_inc(chunk_taken, 1)
                dve.wait_ge(chunk_taken, at(2 * c, t + 1))
                dve.tensor_tensor(merged[:, t], merged[:, t], product[:, t], ALU.add).then_inc(mixed, 1)

            def merged_split(n, bank):
                dve.wait_ge(m_hi, at(2 * n, bank + 1))
                dve.tensor_tensor(mT[1][:, bass.ds(4 * n + 2 * bank, 2)], side[bank][:].rearrange("p (k s) -> p k s", k=2),
                                  mT[0][:, bass.ds(4 * n + 2 * bank, 2)].bitcast(F32), ALU.subtract).then_inc(m_lo, 1)

            def merge(n, attn):
                u0, c = m0 + n * MERGE_U, c0 + 6 * n
                for s in range(MERGE_U):
                    lo(u0, s)
                    if attn:
                        for t in range(TT):
                            if s == U_Z[t] + 1:
                                silu(attn[1], t)
                        attention(*attn, s)
                    else:
                        if s in (2, 3):
                            mix_last(n - 1, s - 2, c - 1)
                        if s in (8, 9):
                            merged_split(n - 1, s - 8)
                    for i in range(3):
                        for t in range(TT):
                            if s == 8 * i + 10 + t:
                                dve.wait_ge(unit_used, at(u0, (i + 1) * CU))
                                dve.wait_ge(gb_in, at(48 * n, 48))
                                if attn:
                                    dve.wait_ge(scores_done if i < 2 else pv_done, 2 * GROUPS)
                                dve.tensor_tensor(gates[i][:, t], acc[i % 2][t][:], gate_b[:, i], ALU.add)\
                                   .then_inc(chunk_taken, 1)
                    if s in (30, 31):
                        t = s - 30
                        dve.wait_ge(unit_used, at(u0, 3 * CU + PROJ_K[0] // UK))
                        dve.wait_ge(gate_tanh, at(6 * n, 2))
                        if attn:
                            dve.wait_ge(ozT_done, 2 * GROUPS)
                        else:
                            dve.wait_ge(mergedT_done, at(2 * n, 0))
                        dve.scalar_tensor_tensor(merged[:, t], gates[0][:, t], 1.0, acc[1][t][:],
                                                 ALU.add, ALU.mult).then_inc(chunk_taken, 1)
                    if s in (36, 37):
                        t = s - 36
                        dve.wait_ge(unit_used, at(u0, MERGE_U - PROJ_K[2] // UK))
                        dve.wait_ge(gate_tanh, at(6 * n, 4))
                        dve.scalar_tensor_tensor(product[:, t], gates[1][:, t], 1.0, acc[0][t][:],
                                                 ALU.add, ALU.mult).then_inc(chunk_taken, 1)
                        dve.wait_ge(chunk_taken, at(2 * c, 9 + t))
                        dve.tensor_tensor(merged[:, t], merged[:, t], product[:, t], ALU.add).then_inc(mixed, 1)

            merge(0, ("ab", GROUPS - 1, OZ_A + 4 * (AB_GROUPS - 1)))
            with dve.Fori(1, NCH) as n:
                merge(n, None)

            u0 = m0 + NCH * MERGE_U
            c = c0 + 6 * NCH

            def result(n, t):
                dve.wait_ge(unit_used, u0 + (n + 1) * CU)
                dve.wait_ge(res_in, 16 * NCH)
                dve.scalar_tensor_tensor(res[n][:, t], acc[n % 2][t][:], 0.5, res[n][:, t], ALU.mult, ALU.add)\
                   .then_inc(chunk_taken, 1)

            for s in range(NCH * CU):
                lo(u0, s)
                if s < TT:
                    mix_last(NCH - 1, s, c - 1)
                if s in (4, 5):
                    merged_split(NCH - 1, s - 4)
                if s >= CU and s % CU in (2, 3):
                    result(s // CU - 1, s % CU - 2)
            for t in range(TT):
                result(NCH - 1, t)

        @block.tensor
        def _(pe):
            def unit(u0, s, x_pair, k, banks, first, last):
                pe.wait_ge(lo_done, at(u0, s + 1))
                for j in range(UK):
                    for t in range(TT):
                        tok = slice(t * P, (t + 1) * P)
                        hi, lo = x_pair[0][:, k + j, tok], x_pair[1][:, k + j, tok]
                        pe.matmul(banks[t][:], hi, whi[:, s % RING, j], start=first and j == 0, stop=False)
                        pe.matmul(banks[t][:], hi, wlo[:, s % RING, j], start=False, stop=False)
                        o = pe.matmul(banks[t][:], lo, whi[:, s % RING, j], start=False, stop=last and j == UK - 1)
                o.then_inc(unit_used, 1)

            def chunk_free(c):
                pe.wait_ge(chunk_taken, at(2 * c, -2))

            def transposes(banks, src, done):
                for blk in range(4):
                    for t in range(TT):
                        c0 = (blk % 2) * S + t * P
                        o = pe.transpose(banks[blk // 2][:, c0:c0 + P], src[:, t, blk * P:(blk + 1) * P], ident)
                    if blk % 2:
                        o.then_inc(done, 1)

            def scores(kind, a, step):
                pe.wait_ge(qkT_evac, at(4 * a, 4))
                if isinstance(a, int) and a == 0:
                    pe.wait_ge(pre["fbias"], 2)
                else:
                    pe.wait_ge(oz_lo, at(2 * a, 0))
                if kind == "m":
                    for t in range(TT):
                        for i in range(2):
                            o = pe.matmul(side[step][:, t * S:(t + 1) * S], qT[:, 2 * step + i, t * P:(t + 1) * P],
                                          kT[:, 2 * step + i], start=i == 0, stop=i == 1)
                else:
                    for h in (2 * step, 2 * step + 1):
                        pe.matmul(side[h][:, 0:S], qT[:, h, P:S], kT[:, h], start=True, stop=True)
                        o = pe.matmul(side[h][:, S:SEG], qT[:, h, 0:P], kT[:, h, 0:P], start=True, stop=True)
                o.then_inc(scores_done, 1)

            def probT(kind, a, step):
                pe.wait_ge(probs_done, at(2 * a, step + 1))
                if kind == "m":
                    for t in range(TT):
                        for k in range(TT):
                            c0 = (2 * t + k) * P
                            o = pe.transpose(side[step][:, c0:c0 + P], probs_m[:, step, t, k * P:(k + 1) * P], ident)
                else:
                    for h in (2 * step, 2 * step + 1):
                        for c0 in range(0, SEG, P):
                            o = pe.transpose(side[h][:, c0:c0 + P], probs[:, h, c0:c0 + P], ident)
                o.then_inc(probT_done, 1)

            def pv(kind, a, step):
                pe.wait_ge(probT_copied, at(2 * a, step + 1))
                pe.wait_ge(chunk_taken, at(8 * a, 6))
                bank = side[step]
                if kind == "m":
                    for t in range(TT):
                        for k in range(TT):
                            o = pe.matmul(bank[:, t * MD:(t + 1) * MD], probs_m[:, step, t, k * P:(k + 1) * P],
                                          v_sb[:, k, step * MD:(step + 1) * MD], start=k == 0, stop=k == 1)
                else:
                    for j in range(2):
                        h = 2 * step + j
                        cols = slice(h * HD, (h + 1) * HD)
                        pe.matmul(bank[:, j * S + P:(j + 1) * S], probs[:, h, 0:P], v_sb[:, 0, cols],
                                  start=True, stop=False)
                        pe.matmul(bank[:, j * S + P:(j + 1) * S], probs[:, h, P:2 * P], v_sb[:, 1, cols],
                                  start=False, stop=True)
                        o = pe.matmul(bank[:, j * S:j * S + P], probs[:, h, 2 * P:], v_sb[:, 0, cols],
                                      start=True, stop=True)
                o.then_inc(pv_done, 1)

            def attention(kind, a, k0, s):
                for step in range(2):
                    if s == S_SCORES[step]:
                        scores(kind, a, step)
                    if s == S_PROBT[step]:
                        probT(kind, a, step)
                if s == S_PV:
                    pv(kind, a, 0)
                    pv(kind, a, 1)
                if s == S_OZT:
                    pe.wait_ge(oz_done, at(2 * a, 2))
                    transposes(side[0:2], silz, ozT_done)

            pe.wait_ge(small_in, 16 * 9)
            pe.wait_ge(pre["rel"], 1)
            pe.matmul(acc[1][1][0:A_HEADS, 0:SEG], rel[:], oh[:], start=True, stop=True).then_inc(pre["dvec"], 1)
            pe.wait_ge(cst_in, 16)
            banks = side + acc[0] + acc[1]
            for t in range(TT):
                pe.wait_ge(pre["xn"], t + 1)
                xk = raw[:, 2 + t].rearrange("p q c -> p (q c)").rearrange("p (i k) -> p k i", k=KT)
                for k in range(KT):
                    if t == 0 and k == KT - 2:
                        pe.wait_ge(pre["dvec_sb"], 1)
                    c0 = (k % 2) * S + t * P
                    o = pe.transpose(banks[k // 2][:, c0:c0 + P], xk[:, k], ident)
                    if t == TT - 1 and k % 2:
                        o.then_inc(pre["xT"], 1)

            def beside_first(s):
                if s in (4, 7):
                    r = (4, 7).index(s)
                    pe.wait_ge(pre["mn"], 2)
                    if r:
                        pe.wait_ge(pre["mT_lo"], 4)
                    for k in range(8 * r, 8 * r + 8):
                        bank = side[(k % 8) // 2]
                        for t in range(TT):
                            mk = mem_sb[:, t].rearrange("p (i k) -> p k i", k=KT)
                            c0 = (k % 2) * S + t * P
                            o = pe.transpose(bank[:, c0:c0 + P], mk[:, k], ident)
                        if k % 2:
                            o.then_inc(pre["mTp"], 1)
                if s == 10:
                    pe.wait_ge(pre["mT_lo"], 8)
                    pe.wait_ge(pre["wf_lo"], 1)
                    for t in range(TT):
                        tok = slice(t * P, (t + 1) * P)
                        dst = side[0][:, t * B_HEADS:(t + 1) * B_HEADS]
                        for k in range(KT):
                            pe.matmul(dst, hT[0][:, k, tok], wf_hi[:, k], start=k == 0, stop=False)
                            pe.matmul(dst, hT[0][:, k, tok], wf_lo[:, k], start=False, stop=False)
                            o = pe.matmul(dst, hT[1][:, k, tok], wf_hi[:, k], start=False, stop=k == KT - 1)
                    o.then_inc(pre["fb"], 1)
                if s == 18:
                    pe.wait_ge(pre["lf"], 1)
                    pe.matmul(side[0][:, 0:B_HEADS], tri[:, 0:P], ls[7][:, 0], start=True, stop=True)
                    pe.matmul(side[0][:, B_HEADS:2 * B_HEADS], tri[:, P:S], ls[7][:, 0], start=True, stop=False)
                    pe.matmul(side[0][:, B_HEADS:2 * B_HEADS], tri[:, 0:P], ls[7][:, 1], start=False, stop=True)\
                      .then_inc(pre["ccol"], 1)
                if s in (20, 26):
                    i = (20, 26).index(s)
                    pe.wait_ge(pre["wtri"], i + 1)
                    pe.wait_ge(*((pre["ccol_sb"], 1) if i == 0 else (pre["fbias"], 1)))
                    for h in range(4):
                        c0 = (h % 2) * S
                        pe.matmul(side[h // 2][:, c0:c0 + S], tri[:, P:S], probs[:, h, 0:S], start=True, stop=False)
                        o = pe.matmul(side[h // 2][:, c0 + P:c0 + S], tri[:, P:S], probs[:, h, S:SEG],
                                      start=False, stop=True)
                    o.then_inc(pre["crow"], 1)

            def body(kind, g, attn):
                u0 = g * BODY_U
                for s in range(BODY_U):
                    w = s // CU
                    if attn is None:
                        beside_first(s)
                    else:
                        attention(*attn, s)
                    for i in range(2):
                        if s == (S_QT, S_KT)[i]:
                            pe.wait_ge(chunk_taken, at(8 * g, 2 * i + 2))
                            if attn is not None:
                                pe.wait_ge(probT_copied, at(2 * g, 0))
                            if i or attn is not None:
                                pe.wait_ge(qkT_evac, at(4 * g, 2 * i))
                            transposes(side[2:4], qn, qkT_done)
                    if s % CU == 0 and (attn is not None or w >= 2):
                        chunk_free(4 * g + w)
                    x_pair = hT
                    if kind == "m" and w in (1, 2):
                        x_pair = mT
                        if attn is None and s == CU:
                            pe.wait_ge(pre["mT_lo"], 4)
                        if attn is None and s == CU + CU // 2:
                            pe.wait_ge(pre["mT_lo"], 8)
                    unit(u0, s, x_pair, UK * (s % CU), acc[w % 2], s % CU == 0, s % CU == CU - 1)

            pe.wait_ge(pre["x_lo"], 8)
            body("m", 0, None)
            body("m", 1, ("m", 0, OZ_M))
            body("ab", 2, ("m", 1, OZ_M + 4))
            with pe.Fori(1, AB_GROUPS) as b:
                body("ab", b + M_GROUPS, ("ab", b + M_GROUPS - 1, OZ_A + 4 * (b - 1)))

            m0 = GROUPS * BODY_U
            c0 = 4 * GROUPS

            def merge(n, attn):
                u0, c = m0 + n * MERGE_U, c0 + 6 * n
                s = 0
                chunks = [(hT, 0, KT)] * 3 + [(ozT, OZ_M, PROJ_K[0]), (ozT, OZ_A, PROJ_K[1]), (ozT, OZ_B, PROJ_K[2])]
                for w, (pair, k0, tiles) in enumerate(chunks):
                    chunk_free(c + w)
                    for k in range(0, tiles, UK):
                        if attn:
                            attention(*attn, s)
                            if w == 3 and k == 0:
                                pe.wait_ge(oz_lo, 2 * GROUPS)
                        elif s == 5:
                            pe.wait_ge(mixed, at(4 * n, 0))
                            transposes(side[0:2], merged, mergedT_done)
                        unit(u0, s, pair, k0 + k, acc[w % 2], k == 0, k == tiles - UK)
                        s += 1

            merge(0, ("ab", GROUPS - 1, OZ_A + 4 * (AB_GROUPS - 1)))
            with pe.Fori(1, NCH) as n:
                merge(n, None)

            u0, c = m0 + NCH * MERGE_U, c0 + 6 * NCH
            for s in range(NCH * CU):
                if s % CU == 0:
                    chunk_free(c + s // CU)
                if s == 4:
                    pe.wait_ge(mixed, 4 * NCH)
                    transposes(side[0:2], merged, mergedT_done)
                if s in (6, 7):
                    pe.wait_ge(m_lo, 2 * NCH - 7 + s)
                unit(u0, s, mT, UK * (s % CU), acc[(s // CU) % 2], s % CU == 0, s % CU == CU - 1)


_INS = ["x", "mem", "norm_g", "mem_norm_g", "w_in", "b_forget", "b_gate", "rel_bias", "q_norm_a", "k_norm_a",
        "q_norm_b", "k_norm_b", "q_norm_m", "k_norm_m", "w_mem_kv", "w_proj_a", "w_proj_b", "w_proj_m", "w_out"]


def shape_constants():
    p, c = np.arange(P)[:, None], np.arange(2 * P)[None, :]
    causal = np.where(c - P > p, MASKED, 0.0)
    consts = np.concatenate([np.eye(P), (c >= p) * 1.0, causal], axis=1).astype(np.float32)
    exact, buckets, far = 16, 32, 2048
    onehot = np.zeros((33, SEG), np.float32)
    for j in range(SEG):
        d = 2 * P - 1 - j
        inside = (0 <= d <= 128) + (d >= 0 and d % 4 == 0 and d <= 512) + (d >= 0 and d % 16 == 0 and d <= 2048)
        if not inside:
            onehot[32, j] = MASKED
            continue
        large = exact + int(np.float32(np.log(np.float32(max(d, 1)) / np.float32(exact))
                                       / np.float32(math.log(far / exact))) * np.float32(buckets - exact))
        onehot[d if d < exact else min(large, buckets - 1), j] = -1.0
        onehot[32, j] = -math.log(inside)
    return consts, onehot


def kernel(**inputs):
    import numpy as _np
    import concourse.bacc as _bacc
    from concourse import mybir as _mybir
    from concourse.bass_utils import run_bass_kernel_spmd as _run

    nc = _bacc.Bacc("TRN2", target_bir_lowering=False, num_devices=1, dynamic_dma_scratch_size=1024)
    arrays, args = {}, []
    consts, onehot = shape_constants()
    named = [(n, inputs[n]) for n in _INS] + [("consts", consts), ("onehot", onehot)]
    for name, value in named:
        a = _np.ascontiguousarray(value)
        arrays[f"in_{name}_dram"] = a
        args.append(nc.dram_tensor(f"in_{name}_dram", a.shape, _mybir.dt.from_np(a.dtype), kind="ExternalInput").ap())
    out = nc.dram_tensor("out_dram", (1, S, D), F32, kind="ExternalOutput").ap()
    hybrid_block(nc, *args, out)
    r = _run(nc, [arrays], core_ids=[0])
    return r.results[0]["out_dram"]
```

```python
import math

import numpy as np

import concourse.bass as bass
from concourse import mybir
from concourse.alu_op_type import AluOpType as ALU

F32 = mybir.dt.float32
F32R = mybir.dt.float32r
ACT = mybir.ActivationFunctionType
AX = mybir.AxisListType

P = 128
D = 2048
S = 256
TT = S // P
KT = D // P
CW = 512
A_HEADS, B_HEADS, M_HEADS, HD, MD = 12, 8, 4, 128, 256
AW, BW, MW = A_HEADS * HD, B_HEADS * HD, M_HEADS * MD
A0 = 0
B0 = 4 * AW
F0 = B0 + 4 * BW
M0 = F0 + B_HEADS
G0 = M0 + 2 * MW
NCOLS = G0 + 3 * D
EPS = 1e-6
MASKED = 1e30

LK = 4
UK = 2
RING = 4
CU = KT // UK
BODY_U = 4 * CU
PROJ_K = (MW // P, AW // P, BW // P)
MERGE_U = 3 * CU + sum(PROJ_K) // UK
M_GROUPS = MW // CW
A_GROUPS = AW // CW
B_GROUPS = BW // CW
AB_GROUPS = A_GROUPS + B_GROUPS
GROUPS = M_GROUPS + AB_GROUPS
NCH = D // CW
OZ_M, OZ_A, OZ_B = 0, PROJ_K[0], PROJ_K[0] + PROJ_K[1]
SEG = 3 * P

S_SCORES = (0, 1)
S_PROBT = (9, 10)
S_PV = 14
S_QT, S_KT = 15, 23
S_OZT = 20
U_Z = (2, 3)
U_LOGITS = (3, 5)
U_PROBS = (4, 6)
U_COPY = (12, 13)
U_OZ = (17, 18)
U_SQ = (10, 18)
U_NORM = (13, 21)
U_EVAC = (18, 26)
U_SPLIT = (23, 24)
U_V = (27, 28)


def last_use(slot, n):
    return max(x for x in range(n) if x % RING == slot)


def x_evac(s):
    return {0: (0,), 1: (1, 2), 2: (3, 4), 3: (5, 6), 4: (7,)}.get(s, ())


def hybrid_block(nc, x, mem, norm_g, mem_norm_g, w_in, b_forget, b_gate, rel_bias,
                 q_norm_a, k_norm_a, q_norm_b, k_norm_b, q_norm_m, k_norm_m,
                 w_mem_kv, w_proj_a, w_proj_b, w_proj_m, w_out, consts, onehot, out):

    def sb(name, shape, dt=F32):
        return nc.alloc_sbuf_tensor(name, shape, dt)

    hT = [sb("hT_hi", [P, KT, S], F32R), sb("hT_lo", [P, KT, S], F32R)]
    mT = [sb("mT_hi", [P, KT, S], F32R), sb("mT_lo", [P, KT, S], F32R)]
    ozT = [sb("ozT_hi", [P, sum(PROJ_K), S], F32R), sb("ozT_lo", [P, sum(PROJ_K), S], F32R)]
    raw = sb("w_raw", [P, RING, LK, CW])
    whi = sb("w_hi", [P, RING, UK, CW], F32R)
    wlo = sb("w_lo", [P, RING, UK, CW], F32R)
    group = sb("group", [P, 8 * 1024])

    def part(at, n):
        return group[:, at:at + n]

    qT = part(0, 1024).rearrange("p (b s) -> p b s", b=4)
    kT = part(1024, 1024).rearrange("p (b s) -> p b s", b=4)
    v_sb = part(2048, 1024).rearrange("p (t c) -> p t c", t=TT)
    silz = part(3072, 1024).rearrange("p (t c) -> p t c", t=TT)
    qn = part(4096, 1024).rearrange("p (t c) -> p t c", t=TT)
    probs = part(5120, 4 * SEG).rearrange("p (h c) -> p h c", h=4)
    probs_m = part(5120, 1024).rearrange("p (h t c) -> p h t c", h=2, t=TT)
    bias = part(5120 + 4 * SEG, 4 * SEG).rearrange("p (h c) -> p h c", h=4)
    mem_sb = part(0, 2 * D).rearrange("p (t c) -> p t c", t=TT)
    waste = part(3 * D, D)
    fbT = part(5120, S)[0:B_HEADS]
    cT = part(5120, S)[0:B_HEADS]
    gates = [part(1024 * i, 1024).rearrange("p (t c) -> p t c", t=TT) for i in range(3)]
    merged, product = silz, qn
    gate_b = part(5120 + 4 * SEG, 3 * CW).rearrange("p (i c) -> p i c", i=3)
    res = [part(0, 1024), part(1024, 1024), part(5120, 1024), part(5120 + 4 * SEG, 1024)]
    res = [r.rearrange("p (t c) -> p t c", t=TT) for r in res]

    cst = sb("cst", [P, P + S + S])
    ident = cst[:, 0:P]
    tri = cst[:, P:P + S]
    causal = cst[:, P + S:P + 2 * S]
    oh = sb("oh", [33, SEG])
    rel = sb("rel", [33, A_HEADS])
    dvec = oh[0:A_HEADS, :]
    gains = sb("gains", [P, 8])
    gq = sb("gq", [P, AB_GROUPS + 2])
    gk = sb("gk", [P, AB_GROUPS + 2])
    gcur = sb("gcur", [P, 2])
    wf = sb("wf", [P, KT, B_HEADS])
    wf_hi, wf_lo = (o[:, 0, 0:KT * B_HEADS].rearrange("p (k h) -> p k h", k=KT) for o in ozT)
    bf = sb("bf", [P, B_HEADS])
    ls = [sb(f"ls{i}", [P, TT, B_HEADS]) for i in range(8)]
    ccol = sb("ccol", [P, TT, B_HEADS])
    half = sb("half", [P, 8])
    gx = sb("gx", [P, KT])
    gm = sb("gm", [P, KT])
    ssx = sb("ssx", [P, 4])
    msx = sb("msx", [P, 4])
    rsx = sb("rsx", [P, 4])
    hrx = sb("hrx", [P, TT])
    ss = sb("ss", [P, 8])
    ms = sb("ms", [P, 8])
    rs = sb("rs", [P, 8])
    rmin = sb("rmin", [P, 8])
    den = sb("den", [P, 8])
    inv = sb("inv", [P, 8])
    spare = sb("spare", [P, 2])
    rden = sb("rden", [P, 8])

    rel_dram = nc.dram_tensor("rel_by_distance", (A_HEADS, SEG), F32, kind="Internal").ap()
    crow_dram = nc.dram_tensor("forget_sums", (B_HEADS, S), F32, kind="Internal").ap()
    bias_dram = nc.dram_tensor("bias_tiles", (AB_GROUPS, P, 4, SEG), F32, kind="Internal").ap()

    acc = [[nc.alloc_psum_tensor(f"acc{c}{t}", [P, CW], F32) for t in range(TT)] for c in range(2)]
    side = [nc.alloc_psum_tensor(f"side{i}", [P, CW], F32) for i in range(4)]

    x_banks = side + acc[1] + side[0:2]

    sem = nc.alloc_semaphore
    load_in = [sem(f"load_in{i}") for i in range(RING)]
    x_in = [sem(f"x_in{i}") for i in range(TT)]
    gx_in, mem_in = sem("gx_in"), sem("mem_in")
    ident_in, cst_in = sem("ident_in"), sem("cst_in")
    small_in, wf_in = sem("small_in"), sem("wf_in")
    hi_done, lo_done, unit_used = sem("hi_done"), sem("lo_done"), sem("unit_used")
    chunk_taken = sem("chunk_taken")
    scores_done, logits_done, probs_done = sem("scores_done"), sem("logits_done"), sem("probs_done")
    probT_done, probT_copied, pv_done = sem("probT_done"), sem("probT_copied"), sem("pv_done")
    inv_done, rden_done, oz_done = sem("inv_done"), sem("rden_done"), sem("oz_done")
    ozT_done, oz_hi, oz_lo = sem("ozT_done"), sem("oz_hi"), sem("oz_lo")
    squares, sums, means, roots = sem("squares"), sem("sums"), sem("means"), sem("roots")
    qkT_done, qkT_evac = sem("qkT_done"), sem("qkT_evac")
    z_tanh, gains_set = sem("z_tanh"), sem("gains_set")
    bias_in, bias_out = sem("bias_in"), sem("bias_out")
    gb_in, gate_tanh = sem("gb_in"), sem("gate_tanh")
    mixed, mergedT_done, m_hi, m_lo = sem("mixed"), sem("mergedT_done"), sem("m_hi"), sem("m_lo")
    res_in, out_sem = sem("res_in"), sem("out_sem")
    pre = {n: sem("pre_" + n) for n in (
        "half rel gains sumx meanx rootx halfx xT x_hi x_lo wf_hi wf_lo dvec dvec_sb dvec_out "
        "summ meanm rootm mTp mT_hi mT_lo "
        "fbT fbT_sb fb v0 v1 vneg e u ln c1 c2 c3 c4 lf ccol ccol_sb crow_sb crow_out crow_in fbias").split()}

    def at(n, k):
        return n + k

    x_v = x.rearrange("b (t p) d -> (b t) p d", p=P)
    mem_v = mem.rearrange("b (t p) d -> (b t) p d", p=P)
    out_v = out.rearrange("b (t p) d -> (b p) t d", p=P)
    x_c = x.rearrange("b (t p) d -> (b p) t d", p=P)
    w_in_v = w_in.rearrange("l (p k) n -> (l p) k n", k=KT)
    w_kv_v = w_mem_kv.rearrange("l (p k) n -> (l p) k n", k=KT)
    w_pa = w_proj_a.rearrange("l (k p) n -> (l p) k n", p=P)
    w_pb = w_proj_b.rearrange("l (k p) n -> (l p) k n", p=P)
    w_pm = w_proj_m.rearrange("l (k p) n -> (l p) k n", p=P)
    w_o = w_out.rearrange("l (k p) n -> (l p) k n", p=P)

    def body_chunks(kind, b):
        if kind == "m":
            return [(w_in_v[:, :, M0:], b * CW), (w_kv_v, b * CW), (w_kv_v[:, :, MW:], b * CW),
                    (w_in_v[:, :, M0 + MW:], b * CW)]
        if kind == "a":
            return [(w_in_v[:, :, A0 + i * AW:], b * CW) for i in range(4)]
        return [(w_in_v[:, :, B0 + i * BW - A_GROUPS * CW:], b * CW) for i in range(4)]

    block = nc.Block()
    with block as block:

        @block.sync
        def _(sp):
            sp.dma_start(ident, consts[:, 0:P]).then_inc(ident_in, 16)
            for t in range(TT):
                sp.dma_start(raw[:, 2 + t].rearrange("p k c -> p (k c)"), x_v[t]).then_inc(x_in[t], 16)

            def load(view, col, k, slot):
                sp.dma_start(raw[:, slot], view[:, k:k + LK, bass.ds(col, CW)]).then_inc(load_in[slot], 16)

            def loads(chunks, u0, before):
                i = 0
                for view, col, tiles in chunks:
                    for k in range(0, tiles, LK):
                        slot = i % RING
                        if i >= RING:
                            sp.wait_ge(lo_done, at(u0, 2 * (i - RING) + 2))
                        elif before is not None:
                            sp.wait_ge(lo_done, at(u0, 2 * (last_use(slot, before) - before) + 2))
                        elif slot >= 2:
                            sp.wait_ge(pre["xT"], 8)
                            sp.wait_ge(pre["sumx"], slot - 1)
                        load(view, col, k, slot)
                        if before is None and i in (1, 3):
                            sp.dma_start(mem_sb[:, i // 2], mem_v[i // 2]).then_inc(mem_in, 16)
                        if before is None and i == 3:
                            sp.dma_start(cst[:, P:], consts[:, P:]).then_inc(cst_in, 16)
                        i += 1

            def body(kind, b, u0, before):
                loads([(w, c, KT) for w, c in body_chunks(kind, b)], u0, before)

            for b in range(M_GROUPS):
                body("m", b, b * BODY_U, None if b == 0 else 2 * CU)
            ab0 = M_GROUPS * BODY_U
            body("a", 0, ab0, 2 * CU)
            with sp.Fori(1, A_GROUPS) as b:
                body("a", b, ab0 + b * BODY_U, 2 * CU)
            with sp.Fori(A_GROUPS, AB_GROUPS) as b:
                body("b", b, ab0 + b * BODY_U, 2 * CU)

            def merge(n, first, u0, before):
                c = (n - first) * CW
                views = [(w_in_v[:, :, G0 + i * D:], KT) for i in (2, 0, 1)]
                views += [(w_pm, PROJ_K[0]), (w_pa, PROJ_K[1]), (w_pb, PROJ_K[2])]
                loads([(w[:, :, first * CW:], c, tiles) for w, tiles in views], u0, before)

            m0 = GROUPS * BODY_U
            merge(0, 0, m0, 2 * CU)
            with sp.Fori(1, NCH) as n:
                merge(n, 1, m0 + n * MERGE_U, MERGE_U // 2)
            loads([(w_o, n * CW, KT) for n in range(NCH)], m0 + NCH * MERGE_U, MERGE_U // 2)

        @block.gpsimd
        def _(pool):
            pool.memset(half[:], -0.5).then_inc(pre["half"], 1)
            pool.wait_ge(pre["half"], 1)
            pool.memset(rel[32:33, :], 1.0).then_inc(pre["rel"], 1)
            pool.wait_ge(pre["rel"], 1)
            pool.wait_ge(pre["meanx"], 1)
            pool.tensor_tensor(rsx[:, 0:2], msx[:, 0:2], half[:, 0:2], ALU.pow).then_inc(pre["rootx"], 1)
            for i in range(2 * M_GROUPS):
                pool.wait_ge(means, i + 1)
                pool.tensor_tensor(rs[:, 0:4], ms[:, 0:4], half[:, 0:4], ALU.pow).then_inc(roots, 1)
                if i == 0:
                    pool.wait_ge(pre["meanm"], 1)
                    pool.wait_ge(pre["rootx"], 1)
                    pool.tensor_tensor(rsx[:, 2:4], msx[:, 2:4], half[:, 0:2], ALU.pow).then_inc(pre["rootm"], 1)
            with pool.Fori(2 * M_GROUPS, 2 * GROUPS) as i:
                pool.wait_ge(means, i + 1)
                pool.tensor_tensor(rs[:], ms[:], half[:], ALU.pow).then_inc(roots, 1)

        @block.scalar
        def _(act):
            def hi(u0, s, lc, before=BODY_U):
                ld = s // 2
                slot = ld % RING
                act.wait_ge(load_in[slot], at(16 * lc[slot], 16 * (ld // RING + 1)))
                if s >= RING:
                    act.wait_ge(unit_used, at(u0, s - RING + 1))
                elif not (isinstance(u0, int) and u0 == 0):
                    act.wait_ge(unit_used, at(u0, last_use(s, before) - before + 1))
                act.activation(whi[:, s % RING], raw[:, slot, UK * (s % 2):UK * (s % 2) + UK], ACT.Copy)\
                   .then_inc(hi_done, 1)

            act.dma_start(gx[:], norm_g.rearrange("l (p k) -> (l p) k", k=KT)).then_inc(gx_in, 16)
            act.dma_start(gm[:], mem_norm_g.rearrange("l (p k) -> (l p) k", k=KT)).then_inc(gx_in, 16)
            with nc.allow_non_contiguous_dma(reason="vectors of a few hundred words, once"):
                for i, (g, w) in enumerate(((q_norm_a, 1), (k_norm_a, 1), (q_norm_b, 1), (k_norm_b, 1),
                                            (q_norm_m, 2), (k_norm_m, 2))):
                    col = i if w == 1 else 4 + 2 * (i - 4)
                    act.dma_start(gains[:, col:col + w], g.rearrange("l (h p) -> p (l h)", p=P))\
                       .then_inc(small_in, 16)
            act.dma_start(rel[0:32, :], rel_bias).then_inc(small_in, 16)
            act.dma_start(oh[:], onehot).then_inc(small_in, 16)
            act.dma_start(bf[:], b_forget.to_broadcast([P, B_HEADS])).then_inc(small_in, 16)
            act.wait_ge(gx_in, 32)
            act.activation(spare[:, 0:1], gx[:, 0:1], ACT.Tanh)

            def tokens_hi(j):
                act.wait_ge(pre["xT"], j + 1)
                for i in range(2):
                    k = 2 * j + i
                    o = act.activation(hT[0][:, k], x_banks[j][:, i * S:(i + 1) * S], ACT.Copy, scale=gx[:, k:k + 1])
                o.then_inc(pre["x_hi"], 1)

            def beside_first(s):
                if s in (12, 13):
                    t = s - 12
                    if t:
                        act.wait_ge(pre["summ"], t)
                    act.activation(waste, mem_sb[:, t], ACT.Square, accum_out=ssx[:, 2 + t:3 + t])\
                       .then_inc(pre["summ"], 1)
                if s == 1:
                    with nc.allow_non_contiguous_dma(reason="eight columns, once"):
                        act.dma_start(wf[:], w_in_v[:, :, F0:F0 + B_HEADS]).then_inc(wf_in, 16)
                for r in range(2):
                    for j in range(4):
                        if s == 7 + 3 * r + j // 2:
                            act.wait_ge(pre["mTp"], 4 * r + j + 1)
                            for i in range(2):
                                k = 8 * r + 2 * j + i
                                o = act.activation(mT[0][:, k], side[j][:, i * S:(i + 1) * S], ACT.Copy,
                                                   scale=gm[:, k:k + 1])
                            o.then_inc(pre["mT_hi"], 1)
                if s == 9:
                    act.wait_ge(wf_in, 16)
                    act.activation(wf_hi, wf[:], ACT.Copy).then_inc(pre["wf_hi"], 1)
                if s == 17:
                    act.wait_ge(pre["vneg"], 1)
                    act.activation(ls[3][:], ls[2][:], ACT.Exp).then_inc(pre["e"], 1)
                if s == 15:
                    act.wait_ge(pre["dvec"], 1)
                    act.activation(dvec, side[2][0:A_HEADS, 0:SEG], ACT.Copy).then_inc(pre["dvec_sb"], 1)
                    act.wait_ge(pre["dvec_sb"], 1)
                    act.dma_start(rel_dram, dvec).then_inc(pre["dvec_out"], 16)
                if s == 19:
                    act.wait_ge(pre["u"], 1)
                    act.activation(ls[5][:], ls[4][:], ACT.Ln).then_inc(pre["ln"], 1)
                if s == 18:
                    act.wait_ge(pre["dvec_out"], 16)
                    for g in range(A_GROUPS):
                        for c0, n, d0 in ((0, 2 * P, 0), (P, P, 2 * P)):
                            src = bass.AP(rel_dram.tensor, g * 4 * SEG + P - 1 + c0, [[SEG, 4], [-1, P], [1, n]])
                            act.dma_start(bias_dram[g, :, :, d0:d0 + n].rearrange("p h c -> h p c"), src)\
                               .then_inc(bias_out, 16)
                if s == 25:
                    act.wait_ge(pre["crow_sb"], 1)
                    act.dma_start(crow_dram, cT).then_inc(pre["crow_out"], 16)
                if s == 27:
                    act.wait_ge(pre["crow_out"], 16)
                    for i in range(B_GROUPS):
                        act.dma_start((bias, probs)[i][:, :, 0:S], crow_dram[4 * i:4 * i + 4].rearrange("(o h) c -> o h c", o=1)
                                      .to_broadcast([P, 4, S])).then_inc(pre["crow_in"], 16)
                if s == 31:
                    for i in range(B_GROUPS):
                        act.wait_ge(pre["fbias"], 2 * i + 2)
                        act.dma_start(bias_dram[A_GROUPS + i], (bias, probs)[i]).then_inc(bias_out, 16)

            def square(kind, w, c, norm, t):
                act.wait_ge(unit_used, CU * c + CU)
                if isinstance(norm, int) and norm == 1:
                    act.wait_ge(pre["rootm"], 1)
                if isinstance(norm, int) and norm == 0:
                    act.wait_ge(pre["rootx"], 1)
                else:
                    act.wait_ge(qkT_done, at(2 * norm, 0))
                r = t + (TT if kind == "m" and w else 0)
                act.activation(qn[:, t], acc[w][t][:], ACT.Square, scale=rsx[:, r:r + 1]).then_inc(squares, 1)

            def z_post(g, t):
                act.wait_ge(unit_used, BODY_U * g + BODY_U)
                if isinstance(g, int) and g == 0:
                    act.wait_ge(pre["halfx"], 1)
                else:
                    act.wait_ge(ozT_done, at(2 * g, 0))
                act.activation(silz[:, t], acc[1][t][:], ACT.Tanh, scale=hrx[:, t:t + 1]).then_inc(z_tanh, 1)

            def evac(kind, norm, which, bank, g):
                dst = (qT, kT)[which]
                act.wait_ge(qkT_done, at(2 * norm, bank + 1))
                if not (isinstance(g, int) and g == 0):
                    act.wait_ge(scores_done, at(2 * g, 0))
                else:
                    act.wait_ge(pre["mTp"], 8)
                act.wait_ge(pre["gains"], 1)
                ps = side[2 + bank]
                if kind == "m":
                    for i in range(2):
                        o = act.activation(dst[:, 2 * bank + i], ps[:, i * S:(i + 1) * S], ACT.Copy,
                                           scale=(gq, gk)[which][:, AB_GROUPS + i:AB_GROUPS + i + 1])
                else:
                    act.wait_ge(gains_set, at(g, 1 - M_GROUPS))
                    o = act.activation(dst[:, 2 * bank:2 * bank + 2], ps[:], ACT.Copy,
                                       scale=gcur[:, which:which + 1])
                o.then_inc(qkT_evac, 1)

            def exps(kind, a, step):
                act.wait_ge(logits_done, at(2 * a, step + 1))
                if kind == "m":
                    if a > 0:
                        act.wait_ge(pv_done, 2 * a)
                    else:
                        act.wait_ge(bias_out, 16 * (2 * A_GROUPS + B_GROUPS))
                    for t in range(TT):
                        i = 2 * step + t
                        o = act.activation(probs_m[:, step, t], side[step][:, t * S:(t + 1) * S], ACT.Exp,
                                           bias=rmin[:, i:i + 1], scale=-1.0, accum_out=den[:, i:i + 1])
                else:
                    for h in (2 * step, 2 * step + 1):
                        for i, c0, n in ((2 * h, 0, 2 * P), (2 * h + 1, 2 * P, P)):
                            o = act.activation(probs[:, h, c0:c0 + n], probs[:, h, c0:c0 + n], ACT.Exp,
                                               bias=rmin[:, i:i + 1], scale=-1.0, accum_out=den[:, i:i + 1])
                o.then_inc(probs_done, 1)

            def split_oz(k0, a, bank):
                act.wait_ge(ozT_done, at(2 * a, bank + 1))
                act.wait_ge(pre["fb"], 1)
                act.activation(ozT[0][:, bass.ds(k0 + 2 * bank, 2)], side[bank][:], ACT.Copy).then_inc(oz_hi, 1)

            def attention(kind, a, k0, s):
                if s in U_PROBS:
                    exps(kind, a, U_PROBS.index(s))
                if s in U_SPLIT:
                    split_oz(k0, a, U_SPLIT.index(s))

            def body(kind, g, b, lc, attn):
                u0 = g * BODY_U
                for s in range(BODY_U):
                    if attn is None:
                        for j in x_evac(s):
                            tokens_hi(j)
                    hi(u0, s, lc)
                    if attn is None:
                        beside_first(s)
                    else:
                        if s in U_Z:
                            z_post(attn[1], U_Z.index(s))
                        attention(*attn, s)
                    for w in range(2):
                        for t in range(TT):
                            if s == U_SQ[w] + t:
                                square(kind, w, 4 * g + w, 2 * g + w, t)
                            if s == U_EVAC[w] + t:
                                evac(kind, 2 * g + w, w, t, g)
                    if attn is not None and kind == "ab" and s == 11:
                        if not (isinstance(b, int) and b == 0):
                            act.wait_ge(logits_done, at(2 * g, 0))
                            act.dma_start(bias, bias_dram[bass.ds(b, 1)].rearrange("g p h c -> (g p) h c"))\
                               .then_inc(bias_in, 16)
                        else:
                            act.wait_ge(bias_out, 16 * (2 * A_GROUPS + B_GROUPS))
                            act.dma_start(bias, bias_dram[0]).then_inc(bias_in, 16)

            per = 2 * CU // RING
            body("m", 0, 0, [0] * 4, None)
            body("m", 1, 1, [per] * 4, ("m", 0, OZ_M))
            body("ab", 2, 0, [2 * per] * 4, ("m", 1, OZ_M + 4))
            with act.Fori(1, AB_GROUPS) as b:
                body("ab", b + M_GROUPS, b, [(b + M_GROUPS) * per] * 4,
                     ("ab", b + M_GROUPS - 1, OZ_A + 4 * (b - 1)))

            m0 = GROUPS * BODY_U
            base = [GROUPS * per] * 4
            merge_l = [len(range(s, MERGE_U // 2, RING)) for s in range(RING)]

            def merged_split(n, bank):
                act.wait_ge(mergedT_done, at(2 * n, bank + 1))
                act.wait_ge(unit_used, M_GROUPS * BODY_U)
                act.activation(mT[0][:, bass.ds(4 * n + 2 * bank, 2)], side[bank][:], ACT.Copy).then_inc(m_hi, 1)

            def merge(n, attn):
                lc = [base[s] + n * merge_l[s] for s in range(RING)]
                for s in range(MERGE_U):
                    hi(m0 + n * MERGE_U, s, lc, BODY_U if attn else MERGE_U)
                    if attn:
                        if s in U_Z:
                            z_post(attn[1], U_Z.index(s))
                        attention(*attn, s)
                    elif s in (8, 9):
                        merged_split(n - 1, s - 8)
                    if s == 7:
                        if attn:
                            act.wait_ge(logits_done, 2 * GROUPS)
                            for i, src in enumerate((2, 0, 1)):
                                act.dma_start(gate_b[:, i], b_gate[0, src:src + 1, 0:CW].to_broadcast([P, CW]))\
                                   .then_inc(gb_in, 16)
                        else:
                            act.wait_ge(chunk_taken, 2 * (4 * GROUPS + 6 * n))
                            for i, src in enumerate((2, 0, 1)):
                                act.dma_start(gate_b[:, i], b_gate[0, src:src + 1, bass.ds(n * CW, CW)]
                                              .to_broadcast([P, CW])).then_inc(gb_in, 16)
                    for i in range(3):
                        for t in range(TT):
                            if s == 8 * i + 11 + t:
                                act.wait_ge(chunk_taken, at(2 * (4 * GROUPS + 6 * n), 2 * i + t + 1))
                                act.activation(gates[i][:, t], gates[i][:, t], ACT.Tanh, scale=0.5)\
                                   .then_inc(gate_tanh, 1)

            merge(0, ("ab", GROUPS - 1, OZ_A + 4 * (AB_GROUPS - 1)))
            with act.Fori(1, NCH) as n:
                merge(n, None)

            lc = [base[s] + NCH * merge_l[s] for s in range(RING)]
            u0 = m0 + NCH * MERGE_U
            act.wait_ge(chunk_taken, 2 * (4 * GROUPS + 6 * NCH - 1))
            for n in range(NCH):
                act.dma_start(res[n], x_c[:, :, n * CW:(n + 1) * CW]).then_inc(res_in, 16)
            for s in range(NCH * CU):
                hi(u0, s, lc, MERGE_U)
                if s in (4, 5):
                    merged_split(NCH - 1, s - 4)
                if s >= CU and s % CU == 5:
                    n = s // CU - 1
                    act.wait_ge(chunk_taken, 2 * (4 * GROUPS + 6 * NCH + n + 1))
                    act.dma_start(out_v[:, :, n * CW:(n + 1) * CW], res[n]).then_inc(out_sem, 16)
            for t in range(TT):
                act.wait_ge(chunk_taken, 2 * (4 * GROUPS + 6 * NCH + NCH - 1) + t + 1)
                act.dma_start(out_v[:, t, (NCH - 1) * CW:], res[NCH - 1][:, t]).then_inc(out_sem, 16)
            act.wait_ge(out_sem, 16 * (NCH + 1))

        @block.vector
        def _(dve):
            def lo(u0, s):
                dve.wait_ge(hi_done, at(u0, s + 1))
                dve.tensor_tensor(wlo[:, s % RING], raw[:, (s // 2) % RING, UK * (s % 2):UK * (s % 2) + UK],
                                  whi[:, s % RING].bitcast(F32), ALU.subtract).then_inc(lo_done, 1)

            def chain(name, n, ins):
                ins.then_inc(pre[name], 1)
                dve.wait_ge(pre[name], n)

            for t in range(TT):
                dve.wait_ge(x_in[t], 16)
                if t:
                    dve.wait_ge(pre["sumx"], t)
                xr = raw[:, 2 + t].rearrange("p k c -> p (k c)")
                dve.tensor_tensor_reduce(out=waste, in0=xr, in1=xr, scale=1.0, scalar=0.0, op0=ALU.mult,
                                         op1=ALU.add, accum_out=ssx[:, t:t + 1]).then_inc(pre["sumx"], 1)
            dve.wait_ge(gx_in, 32)

            def tokens_lo(j):
                dve.wait_ge(pre["x_hi"], j + 1)
                for i in range(2):
                    k = 2 * j + i
                    o = dve.scalar_tensor_tensor(hT[1][:, k], x_banks[j][:, i * S:(i + 1) * S], gx[:, k:k + 1],
                                                 hT[0][:, k].bitcast(F32), ALU.mult, ALU.subtract)
                o.then_inc(pre["x_lo"], 1)

            def norm_sums(g, norm, kind):
                heads, dim = (4, HD) if kind == "ab" else (2, MD)
                dve.wait_ge(squares, at(2 * norm, 2))
                dve.reduce_sum(ss[:, 0:2 * heads], qn.rearrange("p t (h d) -> p (t h) d", d=dim), AX.X)\
                   .then_inc(sums, 1)
                dve.wait_ge(sums, at(norm, 1))
                dve.tensor_scalar(ms[:, 0:2 * heads], ss[:, 0:2 * heads], 1.0 / dim, EPS, ALU.mult, ALU.add)\
                   .then_inc(means, 1)

            def normalise(kind, norm, w, t):
                heads, dim = (4, HD) if kind == "ab" else (2, MD)
                dve.wait_ge(roots, at(norm, 1))
                if isinstance(norm, int) and norm == 1:
                    dve.wait_ge(pre["rootm"], 1)
                r = rs[:, t * heads:(t + 1) * heads].rearrange("p (h o) -> p h o", o=1).to_broadcast([P, heads, dim])
                x = t + (TT if kind == "m" and w else 0)
                dve.scalar_tensor_tensor(qn[:, t].rearrange("p (h d) -> p h d", d=dim),
                                         acc[w][t][:].rearrange("p (h d) -> p h d", d=dim), rsx[:, x:x + 1], r,
                                         ALU.mult, ALU.mult).then_inc(chunk_taken, 1)

            def silu(g, t):
                dve.wait_ge(z_tanh, at(2 * g, t + 1))
                dve.scalar_tensor_tensor(silz[:, t], silz[:, t], 1.0, acc[1][t][:], ALU.add, ALU.mult)\
                   .then_inc(chunk_taken, 1)

            def logits(kind, a, step):
                dve.wait_ge(scores_done, at(2 * a, step + 1))
                if kind == "m":
                    dve.tensor_reduce(rmin[:, 2 * step:2 * step + 2], side[step][:].rearrange("p (t c) -> p t c", t=TT),
                                      AX.X, ALU.min).then_inc(logits_done, 1)
                    return
                dve.wait_ge(bias_in, at(16 * (a - M_GROUPS), 16))
                dve.wait_ge(pv_done, at(2 * a, 0))
                dve.memset(spare[:, step:step + 1], 0.0)
                for h in (2 * step, 2 * step + 1):
                    for i, c0, n in ((2 * h, 0, 2 * P), (2 * h + 1, 2 * P, P)):
                        o = dve.tensor_tensor_reduce(out=probs[:, h, c0:c0 + n], in0=side[h][:, c0:c0 + n],
                                                     in1=bias[:, h, c0:c0 + n], scale=1.0, scalar=3e38,
                                                     op0=ALU.add, op1=ALU.min, accum_out=rmin[:, i:i + 1])
                o.then_inc(logits_done, 1)

            def copy_probT(kind, a, step):
                dve.wait_ge(probT_done, at(2 * a, step + 1))
                if kind == "m":
                    o = dve.tensor_copy(probs_m[:, step].rearrange("p t c -> p (t c)"), side[step][:])
                else:
                    for h in (2 * step, 2 * step + 1):
                        o = dve.tensor_copy(probs[:, h], side[h][:, 0:SEG])
                o.then_inc(probT_copied, 1)

            def half_inverse(kind, a):
                n = 8 if kind == "ab" else 4
                dve.wait_ge(probs_done, at(2 * a, 2))
                dve.reciprocal(inv[:, 0:n], den[:, 0:n]).then_inc(inv_done, 1)
                dve.wait_ge(inv_done, at(a, 1))
                for t in range(TT):
                    first = t if kind == "m" else 1 - t
                    o = dve.tensor_scalar(rden[:, first:n:2], inv[:, first:n:2], hrx[:, t:t + 1], None, ALU.mult)
                o.then_inc(rden_done, 1)

            def gate_output(kind, a, step):
                dve.wait_ge(pv_done, at(2 * a, step + 1))
                dve.wait_ge(rden_done, at(a, 1))
                dve.wait_ge(chunk_taken, at(8 * a, 8))
                for j in range(2):
                    for t in range(TT):
                        if kind == "m":
                            if j:
                                continue
                            i, c0, n, ps = 2 * step + t, step * MD, MD, side[step][:, t * MD:(t + 1) * MD]
                        else:
                            h = 2 * step + j
                            i, c0, n = 2 * h + 1 - t, h * HD, HD
                            ps = side[step][:, j * S + t * P:j * S + (t + 1) * P]
                        o = dve.scalar_tensor_tensor(silz[:, t, c0:c0 + n], ps, rden[:, i:i + 1],
                                                     silz[:, t, c0:c0 + n], ALU.mult, ALU.mult)
                o.then_inc(oz_done, 1)

            def split_oz(k0, a, bank):
                dve.wait_ge(oz_hi, at(2 * a, bank + 1))
                dve.tensor_tensor(ozT[1][:, bass.ds(k0 + 2 * bank, 2)], side[bank][:].rearrange("p (k s) -> p k s", k=2),
                                  ozT[0][:, bass.ds(k0 + 2 * bank, 2)].bitcast(F32), ALU.subtract).then_inc(oz_lo, 1)

            def attention(kind, a, k0, s):
                if s in U_LOGITS:
                    logits(kind, a, U_LOGITS.index(s))
                if s in U_COPY:
                    copy_probT(kind, a, U_COPY.index(s))
                if s == U_COPY[1] + 1:
                    half_inverse(kind, a)
                if s in U_OZ:
                    gate_output(kind, a, U_OZ.index(s))
                if s in U_SPLIT:
                    split_oz(k0, a, U_SPLIT.index(s))

            def forget_bias(i):
                tile = (bias, probs)[i]
                for h in range(4):
                    hh = 4 * i + h
                    o = dve.scalar_tensor_tensor(tile[:, h, 2 * P:], tile[:, h, 0:P], ccol[:, 0, hh:hh + 1],
                                                 causal[:, P:], ALU.subtract, ALU.add)
                o.then_inc(pre["fbias"], 1)
                dve.wait_ge(pre["fbias"], 2 * i + 1)
                for h in range(4):
                    hh = 4 * i + h
                    o = dve.scalar_tensor_tensor(tile[:, h, 0:2 * P], tile[:, h, 0:2 * P], ccol[:, 1, hh:hh + 1],
                                                 causal[:, 0:2 * P], ALU.subtract, ALU.add)
                o.then_inc(pre["fbias"], 1)

            def beside_first(s):
                if s == 4:
                    dve.wait_ge(pre["sumx"], TT)
                    dve.tensor_scalar(msx[:, 0:2], ssx[:, 0:2], 1.0 / D, EPS, ALU.mult, ALU.add)\
                       .then_inc(pre["meanx"], 1)
                    dve.wait_ge(small_in, 16 * 9)
                    for i in range(AB_GROUPS):
                        c = 0 if i < A_GROUPS else 2
                        dve.tensor_scalar(gq[:, i:i + 1], gains[:, c:c + 1], -HD ** -0.5, None, ALU.mult)
                        dve.tensor_copy(gk[:, i:i + 1], gains[:, c + 1:c + 2])
                    dve.tensor_scalar(gq[:, AB_GROUPS:], gains[:, 4:6], -MD ** -0.5, None, ALU.mult)
                    dve.tensor_copy(gk[:, AB_GROUPS:], gains[:, 6:8]).then_inc(pre["gains"], 1)
                if s == 14:
                    dve.wait_ge(pre["summ"], TT)
                    dve.tensor_scalar(msx[:, 2:4], ssx[:, 2:4], 1.0 / D, EPS, ALU.mult, ALU.add)\
                       .then_inc(pre["meanm"], 1)
                if s == 8:
                    dve.wait_ge(pre["rootx"], 1)
                    dve.tensor_scalar(hrx[:], rsx[:, 0:2], 0.5, None, ALU.mult).then_inc(pre["halfx"], 1)
                if s == 9:
                    dve.wait_ge(pre["wf_hi"], 1)
                    dve.tensor_tensor(wf_lo, wf[:], wf_hi.bitcast(F32), ALU.subtract).then_inc(pre["wf_lo"], 1)
                for r in range(2):
                    for j in range(4):
                        if s == 7 + 3 * r + j // 2:
                            dve.wait_ge(pre["mT_hi"], 4 * r + j + 1)
                            for i in range(2):
                                k = 8 * r + 2 * j + i
                                o = dve.scalar_tensor_tensor(mT[1][:, k], side[j][:, i * S:(i + 1) * S],
                                                             gm[:, k:k + 1], mT[0][:, k].bitcast(F32),
                                                             ALU.mult, ALU.subtract)
                            o.then_inc(pre["mT_lo"], 1)
                if s == 14:
                    dve.wait_ge(pre["fbT"], 1)
                    dve.tensor_copy(fbT, side[0][0:B_HEADS, 0:S]).then_inc(pre["fbT_sb"], 1)
                if s == 16:
                    dve.wait_ge(pre["fb"], 1)
                    for t in range(TT):
                        o = dve.scalar_tensor_tensor(ls[0][:, t], side[1][:, t * B_HEADS:(t + 1) * B_HEADS],
                                                     rsx[:, t:t + 1], bf[:], ALU.mult, ALU.add)
                    chain("v0", 1, o)
                    chain("v1", 1, dve.tensor_scalar(ls[1][:], ls[0][:], -1.0, None, ALU.mult))
                    dve.tensor_tensor(ls[2][:], ls[0][:], ls[1][:], ALU.min).then_inc(pre["vneg"], 1)
                if s == 18:
                    dve.wait_ge(pre["e"], 1)
                    dve.tensor_scalar(ls[4][:], ls[3][:], 1.0, None, ALU.add).then_inc(pre["u"], 1)
                if s == 20:
                    dve.wait_ge(pre["ln"], 1)
                    chain("c2", 1, dve.tensor_scalar(ls[1][:], ls[4][:], -1.0, None, ALU.add))
                    chain("c2", 2, dve.tensor_tensor(ls[2][:], ls[3][:], ls[1][:], ALU.subtract))
                    chain("c2", 3, dve.reciprocal(ls[6][:], ls[4][:]))
                    chain("c2", 4, dve.tensor_tensor(ls[1][:], ls[2][:], ls[6][:], ALU.mult))
                    chain("c2", 5, dve.tensor_tensor(ls[2][:], ls[1][:], ls[5][:], ALU.add))
                    chain("c2", 6, dve.tensor_scalar(ls[6][:], ls[0][:], 0.0, None, ALU.min))
                    chain("c2", 7, dve.tensor_tensor(ls[7][:], ls[6][:], ls[2][:], ALU.subtract))
                    dve.tensor_copy(ls[3][:], ls[7][:]).then_inc(pre["lf"], 1)
                if s == 23:
                    dve.wait_ge(pre["ccol"], 1)
                    dve.tensor_copy(ccol[:].rearrange("p t h -> p (t h)"), side[0][:, 0:TT * B_HEADS])\
                       .then_inc(pre["ccol_sb"], 1)
                    dve.tensor_copy(cT, side[1][0:B_HEADS, 0:S]).then_inc(pre["crow_sb"], 1)
                if s in (29, 30):
                    dve.wait_ge(pre["crow_in"], 16 * B_GROUPS)
                    dve.wait_ge(pre["ccol_sb"], 1)
                    dve.wait_ge(cst_in, 16)
                    forget_bias(s - 29)

            def body(kind, g, attn, b=None):
                u0 = g * BODY_U
                for s in range(BODY_U):
                    if attn is None:
                        for j in x_evac(s):
                            tokens_lo(j)
                    lo(u0, s)
                    if s == 9 and kind == "ab":
                        dve.wait_ge(qkT_evac, at(4 * g, 0))
                        dve.wait_ge(pre["gains"], 1)
                        dve.tensor_copy(gcur[:, 0:1], gq[:, bass.ds(b, 1)])
                        dve.tensor_copy(gcur[:, 1:2], gk[:, bass.ds(b, 1)]).then_inc(gains_set, 1)
                    if attn is None:
                        beside_first(s)
                    else:
                        for t in range(TT):
                            if s == U_Z[t] + 1:
                                silu(attn[1], t)
                        attention(*attn, s)
                    for w in range(2):
                        if s == U_SQ[w] + 1:
                            norm_sums(g, 2 * g + w, kind)
                        for t in range(TT):
                            if s == U_NORM[w] + t:
                                normalise(kind, 2 * g + w, w, t)
                    if s in U_V:
                        t = U_V.index(s)
                        dve.wait_ge(unit_used, at(u0, 3 * CU))
                        if attn is not None:
                            dve.wait_ge(pv_done, at(2 * g, 0))
                        else:
                            dve.wait_ge(pre["summ"], TT)
                        r = t + (TT if kind == "m" else 0)
                        dve.tensor_scalar(v_sb[:, t], acc[0][t][:], rsx[:, r:r + 1], None, ALU.mult)\
                           .then_inc(chunk_taken, 1)

            body("m", 0, None)
            body("m", 1, ("m", 0, OZ_M))
            body("ab", 2, ("m", 1, OZ_M + 4), 0)
            with dve.Fori(1, AB_GROUPS) as b:
                body("ab", b + M_GROUPS, ("ab", b + M_GROUPS - 1, OZ_A + 4 * (b - 1)), b)

            m0 = GROUPS * BODY_U
            c0 = 4 * GROUPS

            def mix_last(n, t, c):
                dve.wait_ge(unit_used, m0 + n * MERGE_U + MERGE_U)
                dve.wait_ge(gate_tanh, at(6 * n, 6))
                dve.wait_ge(mixed, at(4 * n, 2))
                dve.scalar_tensor_tensor(product[:, t], gates[2][:, t], 1.0, acc[1][t][:], ALU.add, ALU.mult)\
                   .then_inc(chunk_taken, 1)
                dve.wait_ge(chunk_taken, at(2 * c, t + 1))
                dve.tensor_tensor(merged[:, t], merged[:, t], product[:, t], ALU.add).then_inc(mixed, 1)

            def merged_split(n, bank):
                dve.wait_ge(m_hi, at(2 * n, bank + 1))
                dve.tensor_tensor(mT[1][:, bass.ds(4 * n + 2 * bank, 2)], side[bank][:].rearrange("p (k s) -> p k s", k=2),
                                  mT[0][:, bass.ds(4 * n + 2 * bank, 2)].bitcast(F32), ALU.subtract).then_inc(m_lo, 1)

            def merge(n, attn):
                u0, c = m0 + n * MERGE_U, c0 + 6 * n
                for s in range(MERGE_U):
                    lo(u0, s)
                    if attn:
                        for t in range(TT):
                            if s == U_Z[t] + 1:
                                silu(attn[1], t)
                        attention(*attn, s)
                    else:
                        if s in (2, 3):
                            mix_last(n - 1, s - 2, c - 1)
                        if s in (8, 9):
                            merged_split(n - 1, s - 8)
                    for i in range(3):
                        for t in range(TT):
                            if s == 8 * i + 10 + t:
                                dve.wait_ge(unit_used, at(u0, (i + 1) * CU))
                                dve.wait_ge(gb_in, at(48 * n, 48))
                                if attn:
                                    dve.wait_ge(scores_done if i < 2 else pv_done, 2 * GROUPS)
                                dve.scalar_tensor_tensor(gates[i][:, t], acc[i % 2][t][:], rsx[:, t:t + 1],
                                                         gate_b[:, i], ALU.mult, ALU.add)\
                                   .then_inc(chunk_taken, 1)
                    if s in (30, 31):
                        t = s - 30
                        dve.wait_ge(unit_used, at(u0, 3 * CU + PROJ_K[0] // UK))
                        dve.wait_ge(gate_tanh, at(6 * n, 2))
                        if attn:
                            dve.wait_ge(ozT_done, 2 * GROUPS)
                        else:
                            dve.wait_ge(mergedT_done, at(2 * n, 0))
                        dve.scalar_tensor_tensor(merged[:, t], gates[0][:, t], 1.0, acc[1][t][:],
                                                 ALU.add, ALU.mult).then_inc(chunk_taken, 1)
                    if s in (36, 37):
                        t = s - 36
                        dve.wait_ge(unit_used, at(u0, MERGE_U - PROJ_K[2] // UK))
                        dve.wait_ge(gate_tanh, at(6 * n, 4))
                        dve.scalar_tensor_tensor(product[:, t], gates[1][:, t], 1.0, acc[0][t][:],
                                                 ALU.add, ALU.mult).then_inc(chunk_taken, 1)
                        dve.wait_ge(chunk_taken, at(2 * c, 9 + t))
                        dve.tensor_tensor(merged[:, t], merged[:, t], product[:, t], ALU.add).then_inc(mixed, 1)

            merge(0, ("ab", GROUPS - 1, OZ_A + 4 * (AB_GROUPS - 1)))
            with dve.Fori(1, NCH) as n:
                merge(n, None)

            u0 = m0 + NCH * MERGE_U
            c = c0 + 6 * NCH

            def result(n, t):
                dve.wait_ge(unit_used, u0 + (n + 1) * CU)
                dve.wait_ge(res_in, 16 * NCH)
                dve.scalar_tensor_tensor(res[n][:, t], acc[n % 2][t][:], 0.5, res[n][:, t], ALU.mult, ALU.add)\
                   .then_inc(chunk_taken, 1)

            for s in range(NCH * CU):
                lo(u0, s)
                if s < TT:
                    mix_last(NCH - 1, s, c - 1)
                if s in (4, 5):
                    merged_split(NCH - 1, s - 4)
                if s >= CU and s % CU in (2, 3):
                    result(s // CU - 1, s % CU - 2)
            for t in range(TT):
                result(NCH - 1, t)

        @block.tensor
        def _(pe):
            def unit(u0, s, x_pair, k, banks, first, last):
                pe.wait_ge(lo_done, at(u0, s + 1))
                for j in range(UK):
                    for t in range(TT):
                        tok = slice(t * P, (t + 1) * P)
                        hi, lo = x_pair[0][:, k + j, tok], x_pair[1][:, k + j, tok]
                        pe.matmul(banks[t][:], hi, whi[:, s % RING, j], start=first and j == 0, stop=False)
                        pe.matmul(banks[t][:], hi, wlo[:, s % RING, j], start=False, stop=False)
                        o = pe.matmul(banks[t][:], lo, whi[:, s % RING, j], start=False, stop=last and j == UK - 1)
                o.then_inc(unit_used, 1)

            def chunk_free(c):
                pe.wait_ge(chunk_taken, at(2 * c, -2))

            def transposes(banks, src, done):
                for blk in range(4):
                    for t in range(TT):
                        c0 = (blk % 2) * S + t * P
                        o = pe.transpose(banks[blk // 2][:, c0:c0 + P], src[:, t, blk * P:(blk + 1) * P], ident)
                    if blk % 2:
                        o.then_inc(done, 1)

            def scores(kind, a, step):
                pe.wait_ge(qkT_evac, at(4 * a, 4))
                if isinstance(a, int) and a == 0:
                    pe.wait_ge(pre["crow_sb"], 1)
                else:
                    pe.wait_ge(oz_lo, at(2 * a, 0))
                if kind == "m":
                    for t in range(TT):
                        for i in range(2):
                            o = pe.matmul(side[step][:, t * S:(t + 1) * S], qT[:, 2 * step + i, t * P:(t + 1) * P],
                                          kT[:, 2 * step + i], start=i == 0, stop=i == 1)
                else:
                    for h in (2 * step, 2 * step + 1):
                        pe.matmul(side[h][:, 0:S], qT[:, h, P:S], kT[:, h], start=True, stop=True)
                        o = pe.matmul(side[h][:, S:SEG], qT[:, h, 0:P], kT[:, h, 0:P], start=True, stop=True)
                o.then_inc(scores_done, 1)

            def probT(kind, a, step):
                pe.wait_ge(probs_done, at(2 * a, step + 1))
                if kind == "m":
                    for t in range(TT):
                        for k in range(TT):
                            c0 = (2 * t + k) * P
                            o = pe.transpose(side[step][:, c0:c0 + P], probs_m[:, step, t, k * P:(k + 1) * P], ident)
                else:
                    for h in (2 * step, 2 * step + 1):
                        for c0 in range(0, SEG, P):
                            o = pe.transpose(side[h][:, c0:c0 + P], probs[:, h, c0:c0 + P], ident)
                o.then_inc(probT_done, 1)

            def pv(kind, a, step):
                pe.wait_ge(probT_copied, at(2 * a, step + 1))
                pe.wait_ge(chunk_taken, at(8 * a, 6))
                bank = side[step]
                if kind == "m":
                    for t in range(TT):
                        for k in range(TT):
                            o = pe.matmul(bank[:, t * MD:(t + 1) * MD], probs_m[:, step, t, k * P:(k + 1) * P],
                                          v_sb[:, k, step * MD:(step + 1) * MD], start=k == 0, stop=k == 1)
                else:
                    for j in range(2):
                        h = 2 * step + j
                        cols = slice(h * HD, (h + 1) * HD)
                        pe.matmul(bank[:, j * S + P:(j + 1) * S], probs[:, h, 0:P], v_sb[:, 0, cols],
                                  start=True, stop=False)
                        pe.matmul(bank[:, j * S + P:(j + 1) * S], probs[:, h, P:2 * P], v_sb[:, 1, cols],
                                  start=False, stop=True)
                        o = pe.matmul(bank[:, j * S:j * S + P], probs[:, h, 2 * P:], v_sb[:, 0, cols],
                                      start=True, stop=True)
                o.then_inc(pv_done, 1)

            def attention(kind, a, k0, s):
                for step in range(2):
                    if s == S_SCORES[step]:
                        scores(kind, a, step)
                    if s == S_PROBT[step]:
                        probT(kind, a, step)
                if s == S_PV:
                    pv(kind, a, 0)
                    pv(kind, a, 1)
                if s == S_OZT:
                    pe.wait_ge(oz_done, at(2 * a, 2))
                    transposes(side[0:2], silz, ozT_done)

            def tokens_T(t, js):
                xk = raw[:, 2 + t].rearrange("p q c -> p (q c)").rearrange("p (i k) -> p k i", k=KT)
                for j in js:
                    if j >= 6 and t == 0:
                        pe.wait_ge(pre["x_lo"], j - 5)
                    for i in range(2):
                        c0 = i * S + t * P
                        o = pe.transpose(x_banks[j][:, c0:c0 + P], xk[:, 2 * j + i], ident)
                    if t == TT - 1:
                        o.then_inc(pre["xT"], 1)

            pe.wait_ge(ident_in, 16)
            for t in range(TT):
                pe.wait_ge(x_in[t], 16)
                tokens_T(t, range(6))

            def beside_first(s):
                if s == 1:
                    for t in range(TT):
                        tokens_T(t, range(6, 8))
                if s in (6, 9):
                    r = (6, 9).index(s)
                    pe.wait_ge(mem_in, 16 * TT)
                    pe.wait_ge(*((pre["mT_lo"], 4) if r else (pre["x_lo"], 8)))
                    for k in range(8 * r, 8 * r + 8):
                        bank = side[(k % 8) // 2]
                        for t in range(TT):
                            mk = mem_sb[:, t].rearrange("p (i k) -> p k i", k=KT)
                            c0 = (k % 2) * S + t * P
                            o = pe.transpose(bank[:, c0:c0 + P], mk[:, k], ident)
                        if k % 2:
                            o.then_inc(pre["mTp"], 1)
                if s == 12:
                    pe.wait_ge(pre["mT_lo"], 8)
                    pe.wait_ge(pre["wf_lo"], 1)
                    for k in range(KT):
                        dst = side[0][0:B_HEADS, 0:S]
                        pe.matmul(dst, wf_hi[:, k], hT[0][:, k], start=k == 0, stop=False)
                        pe.matmul(dst, wf_hi[:, k], hT[1][:, k], start=False, stop=False)
                        o = pe.matmul(dst, wf_lo[:, k], hT[0][:, k], start=False, stop=k == KT - 1)
                    o.then_inc(pre["fbT"], 1)
                if s == 13:
                    pe.wait_ge(small_in, 16 * 9)
                    pe.wait_ge(pre["rel"], 1)
                    pe.matmul(side[2][0:A_HEADS, 0:SEG], rel[:], oh[:], start=True, stop=True)\
                      .then_inc(pre["dvec"], 1)
                if s == 15:
                    pe.wait_ge(pre["fbT_sb"], 1)
                    for t in range(TT):
                        o = pe.transpose(side[1][:, t * B_HEADS:(t + 1) * B_HEADS], fbT[:, t * P:(t + 1) * P],
                                         ident[0:B_HEADS, 0:B_HEADS])
                    o.then_inc(pre["fb"], 1)
                    pe.wait_ge(pre["dvec_sb"], 1)
                if s == 22:
                    pe.wait_ge(cst_in, 16)
                    pe.wait_ge(pre["lf"], 1)
                    pe.matmul(side[0][:, 0:B_HEADS], tri[:, 0:P], ls[7][:, 0], start=True, stop=True)
                    pe.matmul(side[0][:, B_HEADS:2 * B_HEADS], tri[:, P:S], ls[7][:, 0], start=True, stop=False)
                    pe.matmul(side[0][:, B_HEADS:2 * B_HEADS], tri[:, 0:P], ls[7][:, 1], start=False, stop=True)
                    pe.matmul(side[1][0:B_HEADS, 0:S], ls[7][:, 0], tri, start=True, stop=False)
                    pe.matmul(side[1][0:B_HEADS, P:S], ls[7][:, 1], tri[:, 0:P], start=False, stop=True)\
                      .then_inc(pre["ccol"], 1)

            def body(kind, g, attn):
                u0 = g * BODY_U
                for s in range(BODY_U):
                    w = s // CU
                    if attn is None:
                        beside_first(s)
                    else:
                        attention(*attn, s)
                    for i in range(2):
                        if s == (S_QT, S_KT)[i]:
                            pe.wait_ge(chunk_taken, at(8 * g, 2 * i + 2))
                            if attn is not None:
                                pe.wait_ge(probT_copied, at(2 * g, 0))
                            if i or attn is not None:
                                pe.wait_ge(qkT_evac, at(4 * g, 2 * i))
                            transposes(side[2:4], qn, qkT_done)
                    if s % CU == 0 and (attn is not None or w >= 2):
                        chunk_free(4 * g + w)
                    if attn is None and s < CU:
                        pe.wait_ge(pre["x_lo"], s + 1)
                    x_pair = hT
                    if kind == "m" and w in (1, 2):
                        x_pair = mT
                        if attn is None and s == CU:
                            pe.wait_ge(pre["mT_lo"], 4)
                        if attn is None and s == CU + CU // 2:
                            pe.wait_ge(pre["mT_lo"], 8)
                    unit(u0, s, x_pair, UK * (s % CU), acc[w % 2], s % CU == 0, s % CU == CU - 1)

            body("m", 0, None)
            body("m", 1, ("m", 0, OZ_M))
            body("ab", 2, ("m", 1, OZ_M + 4))
            with pe.Fori(1, AB_GROUPS) as b:
                body("ab", b + M_GROUPS, ("ab", b + M_GROUPS - 1, OZ_A + 4 * (b - 1)))

            m0 = GROUPS * BODY_U
            c0 = 4 * GROUPS

            def merge(n, attn):
                u0, c = m0 + n * MERGE_U, c0 + 6 * n
                s = 0
                chunks = [(hT, 0, KT)] * 3 + [(ozT, OZ_M, PROJ_K[0]), (ozT, OZ_A, PROJ_K[1]), (ozT, OZ_B, PROJ_K[2])]
                for w, (pair, k0, tiles) in enumerate(chunks):
                    chunk_free(c + w)
                    for k in range(0, tiles, UK):
                        if attn:
                            attention(*attn, s)
                            if w == 3 and k == 0:
                                pe.wait_ge(oz_lo, 2 * GROUPS)
                        elif s == 5:
                            pe.wait_ge(mixed, at(4 * n, 0))
                            transposes(side[0:2], merged, mergedT_done)
                        unit(u0, s, pair, k0 + k, acc[w % 2], k == 0, k == tiles - UK)
                        s += 1

            merge(0, ("ab", GROUPS - 1, OZ_A + 4 * (AB_GROUPS - 1)))
            with pe.Fori(1, NCH) as n:
                merge(n, None)

            u0, c = m0 + NCH * MERGE_U, c0 + 6 * NCH
            for s in range(NCH * CU):
                if s % CU == 0:
                    chunk_free(c + s // CU)
                if s == 4:
                    pe.wait_ge(mixed, 4 * NCH)
                    transposes(side[0:2], merged, mergedT_done)
                if s in (6, 7):
                    pe.wait_ge(m_lo, 2 * NCH - 7 + s)
                unit(u0, s, mT, UK * (s % CU), acc[(s // CU) % 2], s % CU == 0, s % CU == CU - 1)


_INS = ["x", "mem", "norm_g", "mem_norm_g", "w_in", "b_forget", "b_gate", "rel_bias", "q_norm_a", "k_norm_a",
        "q_norm_b", "k_norm_b", "q_norm_m", "k_norm_m", "w_mem_kv", "w_proj_a", "w_proj_b", "w_proj_m", "w_out"]


def shape_constants():
    p, c = np.arange(P)[:, None], np.arange(2 * P)[None, :]
    causal = np.where(c - P > p, MASKED, 0.0)
    consts = np.concatenate([np.eye(P), (c >= p) * 1.0, causal], axis=1).astype(np.float32)
    exact, buckets, far = 16, 32, 2048
    onehot = np.zeros((33, SEG), np.float32)
    for j in range(SEG):
        d = 2 * P - 1 - j
        inside = (0 <= d <= 128) + (d >= 0 and d % 4 == 0 and d <= 512) + (d >= 0 and d % 16 == 0 and d <= 2048)
        if not inside:
            onehot[32, j] = MASKED
            continue
        large = exact + int(np.float32(np.log(np.float32(max(d, 1)) / np.float32(exact))
                                       / np.float32(math.log(far / exact))) * np.float32(buckets - exact))
        onehot[d if d < exact else min(large, buckets - 1), j] = -1.0
        onehot[32, j] = -math.log(inside)
    return consts, onehot


def kernel(**inputs):
    import numpy as _np
    import concourse.bacc as _bacc
    from concourse import mybir as _mybir
    from concourse.bass_utils import run_bass_kernel_spmd as _run

    nc = _bacc.Bacc("TRN2", target_bir_lowering=False, num_devices=1, dynamic_dma_scratch_size=1024)
    arrays, args = {}, []
    consts, onehot = shape_constants()
    named = [(n, inputs[n]) for n in _INS] + [("consts", consts), ("onehot", onehot)]
    for name, value in named:
        a = _np.ascontiguousarray(value)
        arrays[f"in_{name}_dram"] = a
        args.append(nc.dram_tensor(f"in_{name}_dram", a.shape, _mybir.dt.from_np(a.dtype), kind="ExternalInput").ap())
    out = nc.dram_tensor("out_dram", (1, S, D), F32, kind="ExternalOutput").ap()
    hybrid_block(nc, *args, out)
    r = _run(nc, [arrays], core_ids=[0])
    return r.results[0]["out_dram"]
```

```python
import math

import numpy as np

import concourse.bass as bass
from concourse import mybir
from concourse.alu_op_type import AluOpType as ALU

F32 = mybir.dt.float32
F32R = mybir.dt.float32r
ACT = mybir.ActivationFunctionType
AX = mybir.AxisListType

P = 128
D = 2048
S = 256
TT = S // P
KT = D // P
CW = 512
A_HEADS, B_HEADS, M_HEADS, HD, MD = 12, 8, 4, 128, 256
AW, BW, MW = A_HEADS * HD, B_HEADS * HD, M_HEADS * MD
B0 = 4 * AW
F0 = B0 + 4 * BW
M0 = F0 + B_HEADS
G0 = M0 + 2 * MW
EPS = 1e-6
MASKED = 1e30

LK = 4
UK = 2
RING = 4
CU = KT // UK
BODY_U = 4 * CU
PROJ_K = (MW // P, AW // P, BW // P)
MERGE_U = 3 * CU + sum(PROJ_K) // UK
M_GROUPS = MW // CW
A_GROUPS = AW // CW
B_GROUPS = BW // CW
AB_GROUPS = A_GROUPS + B_GROUPS
GROUPS = M_GROUPS + AB_GROUPS
NCH = D // CW
OZ_M, OZ_A, OZ_B = 0, PROJ_K[0], PROJ_K[0] + PROJ_K[1]
SEG = 3 * P

S_SCORES = (0, 1)
S_PROBT = (9, 10)
S_PV = 14
S_QT, S_KT = 15, 23
S_OZT = 20
U_Z = (2, 3)
U_LOGITS = (3, 5)
U_PROBS = (4, 6)
U_COPY = (12, 13)
U_OZ = (17, 18)
U_SQ = (10, 18)
U_NORM = (13, 21)
U_EVAC = (18, 26)
U_SPLIT = (23, 24)
U_V = (27, 28)


def last_use(slot, n):
    return max(x for x in range(n) if x % RING == slot)


def fixed(n, value):
    return isinstance(n, int) and n == value


def x_evac(s):
    return {0: (0, 1), 1: (2,), 2: (3, 4), 3: (5,), 4: (6,), 5: (7,)}.get(s, ())


def hybrid_block(nc, x, mem, norm_g, mem_norm_g, w_in, b_forget, b_gate, rel_bias,
                 q_norm_a, k_norm_a, q_norm_b, k_norm_b, q_norm_m, k_norm_m,
                 w_mem_kv, w_proj_a, w_proj_b, w_proj_m, w_out, consts, onehot, out):

    def sb(name, shape, dt=F32):
        return nc.alloc_sbuf_tensor(name, shape, dt)

    hT = [sb("hT_hi", [P, KT, S], F32R), sb("hT_lo", [P, KT, S], F32R)]
    mT = [sb("mT_hi", [P, KT, S], F32R), sb("mT_lo", [P, KT, S], F32R)]
    ozT = [sb("ozT_hi", [P, sum(PROJ_K), S], F32R), sb("ozT_lo", [P, sum(PROJ_K), S], F32R)]
    raw = sb("w_raw", [P, RING, LK, CW])
    whi = sb("w_hi", [P, RING, UK, CW], F32R)
    wlo = sb("w_lo", [P, RING, UK, CW], F32R)
    group = sb("group", [P, 8 * 1024])

    def part(at, n):
        return group[:, at:at + n]

    qT = part(0, 1024).rearrange("p (b s) -> p b s", b=4)
    kT = part(1024, 1024).rearrange("p (b s) -> p b s", b=4)
    v_sb = part(2048, 1024).rearrange("p (t c) -> p t c", t=TT)
    silz = part(3072, 1024).rearrange("p (t c) -> p t c", t=TT)
    qn = part(4096, 1024).rearrange("p (t c) -> p t c", t=TT)
    probs = part(5120, 4 * SEG).rearrange("p (h c) -> p h c", h=4)
    probs_m = part(5120, 1024).rearrange("p (h t c) -> p h t c", h=2, t=TT)
    bias = part(5120 + 4 * SEG, 4 * SEG).rearrange("p (h c) -> p h c", h=4)
    mem_sb = part(0, 2 * D).rearrange("p (t c) -> p t c", t=TT)
    waste = part(3 * D, D)
    fbT = part(5120, S)[0:B_HEADS]
    cT = part(5120, S)[0:B_HEADS]
    gates = [part(1024 * i, 1024).rearrange("p (t c) -> p t c", t=TT) for i in range(3)]
    merged, product = silz, qn
    gate_b = part(5120 + 4 * SEG, 3 * CW).rearrange("p (i c) -> p i c", i=3)
    res = [part(0, 1024), part(1024, 1024), part(5120, 1024), part(5120 + 4 * SEG, 1024)]
    res = [r.rearrange("p (t c) -> p t c", t=TT) for r in res]

    cst = sb("cst", [P, P + S + S])
    ident = cst[:, 0:P]
    tri = cst[:, P:P + S]
    causal = cst[:, P + S:P + 2 * S]
    oh = sb("oh", [33, SEG])
    rel = sb("rel", [33, A_HEADS])
    dvec = oh[0:A_HEADS, :]
    gains = sb("gains", [P, 8])
    gq = sb("gq", [P, AB_GROUPS + 2])
    gk = sb("gk", [P, AB_GROUPS + 2])
    gcur = sb("gcur", [P, 2])
    wf = sb("wf", [P, KT, B_HEADS])
    wf_hi, wf_lo = (o[:, 0, 0:KT * B_HEADS].rearrange("p (k h) -> p k h", k=KT) for o in ozT)
    bf = sb("bf", [P, B_HEADS])
    ls = [sb(f"ls{i}", [P, TT, B_HEADS]) for i in range(8)]
    ccol = sb("ccol", [P, TT, B_HEADS])
    half = sb("half", [P, 8])
    gx = sb("gx", [P, KT])
    gm = sb("gm", [P, KT])
    sqx = sb("sqx", [P, 3])
    ssx = sb("ssx", [P, 4])
    msx = sb("msx", [P, 4])
    rsx = sb("rsx", [P, 4])
    hrx = sb("hrx", [P, TT])
    ss = sb("ss", [P, 8])
    ms = sb("ms", [P, 8])
    rs = sb("rs", [P, 8])
    rmin = sb("rmin", [P, 8])
    den = sb("den", [P, 8])
    inv = sb("inv", [P, 8])
    spare = sb("spare", [P, 2])
    rden = sb("rden", [P, 8])

    rel_dram = nc.dram_tensor("rel_by_distance", (A_HEADS, SEG), F32, kind="Internal").ap()
    crow_dram = nc.dram_tensor("forget_sums", (B_HEADS, S), F32, kind="Internal").ap()
    bias_dram = nc.dram_tensor("bias_tiles", (AB_GROUPS, P, 4, SEG), F32, kind="Internal").ap()

    acc = [[nc.alloc_psum_tensor(f"acc{c}{t}", [P, CW], F32) for t in range(TT)] for c in range(2)]
    side = [nc.alloc_psum_tensor(f"side{i}", [P, CW], F32) for i in range(4)]

    x_banks = side + acc[1] + side[0:2]

    sem = nc.alloc_semaphore
    load_in = [sem(f"load_in{i}") for i in range(RING)]
    x_in = [sem(f"x_in{i}") for i in range(TT)]
    first_half_in = sem("first_half_in")
    gx_in, mem_in = sem("gx_in"), sem("mem_in")
    ident_in, cst_in = sem("ident_in"), sem("cst_in")
    small_in, wf_in = sem("small_in"), sem("wf_in")
    hi_done, lo_done, unit_used = sem("hi_done"), sem("lo_done"), sem("unit_used")
    tail_done = sem("tail_done")
    chunk_taken = sem("chunk_taken")
    scores_done, logits_done, probs_done = sem("scores_done"), sem("logits_done"), sem("probs_done")
    probT_done, probT_copied, pv_done = sem("probT_done"), sem("probT_copied"), sem("pv_done")
    inv_done, rden_done, oz_done = sem("inv_done"), sem("rden_done"), sem("oz_done")
    ozT_done, oz_hi, oz_lo = sem("ozT_done"), sem("oz_hi"), sem("oz_lo")
    squares, sums, means, roots = sem("squares"), sem("sums"), sem("means"), sem("roots")
    qkT_done, qkT_evac = sem("qkT_done"), sem("qkT_evac")
    z_tanh, gains_set = sem("z_tanh"), sem("gains_set")
    bias_in, bias_out = sem("bias_in"), sem("bias_out")
    gb_in, gate_tanh = sem("gb_in"), sem("gate_tanh")
    mixed, mergedT_done, m_hi, m_lo = sem("mixed"), sem("mergedT_done"), sem("m_hi"), sem("m_lo")
    res_in, out_sem = sem("res_in"), sem("out_sem")
    pre = {n: sem("pre_" + n) for n in (
        "half rel gains sumx meanx rootx halfx xT x_hi x_lo wf_hi wf_lo dvec dvec_sb dvec_out "
        "summ meanm rootm mTp mT_hi mT_lo "
        "fbT fbT_sb fb v0 v1 vneg e u ln log1p lf ccol ccol_sb crow_sb crow_out crow_in fbias").split()}

    x_v = x.rearrange("b (t p) d -> (b t) p d", p=P)
    mem_v = mem.rearrange("b (t p) d -> (b t) p d", p=P)
    out_v = out.rearrange("b (t p) d -> (b p) t d", p=P)
    x_c = x.rearrange("b (t p) d -> (b p) t d", p=P)
    w_in_v = w_in.rearrange("l (p k) n -> (l p) k n", k=KT)
    w_kv_v = w_mem_kv.rearrange("l (p k) n -> (l p) k n", k=KT)
    w_pa = w_proj_a.rearrange("l (k p) n -> (l p) k n", p=P)
    w_pb = w_proj_b.rearrange("l (k p) n -> (l p) k n", p=P)
    w_pm = w_proj_m.rearrange("l (k p) n -> (l p) k n", p=P)
    w_o = w_out.rearrange("l (k p) n -> (l p) k n", p=P)

    def body_chunks(kind, b):
        if kind == "m":
            return [(w_in_v[:, :, M0:], b * CW), (w_kv_v, b * CW), (w_kv_v[:, :, MW:], b * CW),
                    (w_in_v[:, :, M0 + MW:], b * CW)]
        if kind == "a":
            return [(w_in_v[:, :, i * AW:], b * CW) for i in range(4)]
        return [(w_in_v[:, :, B0 + i * BW - A_GROUPS * CW:], b * CW) for i in range(4)]

    block = nc.Block()
    with block as block:

        @block.sync
        def _(sp):
            sp.dma_start(ident, consts[:, 0:P]).then_inc(ident_in, 16)

            def load(view, col, k, slot):
                sp.dma_start(raw[:, slot], view[:, k:k + LK, bass.ds(col, CW)]).then_inc(load_in[slot], 16)

            def loads(chunks, u0, before):
                i = 0
                for view, col, tiles in chunks:
                    for k in range(0, tiles, LK):
                        slot = i % RING
                        if i >= RING:
                            sp.wait_ge(lo_done, u0 + 2 * (i - RING) + 2)
                        elif before is not None:
                            sp.wait_ge(lo_done, u0 + 2 * (last_use(slot, before) - before) + 2)
                        elif slot >= 2:
                            sp.wait_ge(pre["xT"], 8)
                            sp.wait_ge(pre["sumx"], (1, 3)[slot - 2])
                        if before is None and i == 0:
                            for t in range(TT):
                                sp.dma_start(raw[:, 2 + t].rearrange("p k c -> p (k c)"), x_v[t])\
                                  .then_inc(x_in[t], 16)
                                tiles_t = slice(UK * t, UK * t + UK)
                                sp.dma_start(raw[:, slot, tiles_t], view[:, tiles_t, bass.ds(col, CW)])\
                                  .then_inc((first_half_in, load_in[slot])[t], 16)
                        else:
                            load(view, col, k, slot)
                        if before is None and i in (1, 3):
                            sp.dma_start(mem_sb[:, i // 2], mem_v[i // 2]).then_inc(mem_in, 16)
                        if before is None and i == 3:
                            sp.dma_start(cst[:, P:], consts[:, P:]).then_inc(cst_in, 16)
                        i += 1

            def body(kind, b, u0, before):
                loads([(w, c, KT) for w, c in body_chunks(kind, b)], u0, before)

            for b in range(M_GROUPS):
                body("m", b, b * BODY_U, None if b == 0 else 2 * CU)
            ab0 = M_GROUPS * BODY_U
            body("a", 0, ab0, 2 * CU)
            with sp.Fori(1, A_GROUPS) as b:
                body("a", b, ab0 + b * BODY_U, 2 * CU)
            with sp.Fori(A_GROUPS, AB_GROUPS) as b:
                body("b", b, ab0 + b * BODY_U, 2 * CU)

            def merge(n, first, u0, before):
                c = (n - first) * CW
                views = [(w_in_v[:, :, G0 + i * D:], KT) for i in (2, 0, 1)]
                views += [(w_pm, PROJ_K[0]), (w_pa, PROJ_K[1]), (w_pb, PROJ_K[2])]
                loads([(w[:, :, first * CW:], c, tiles) for w, tiles in views], u0, before)

            m0 = GROUPS * BODY_U
            merge(0, 0, m0, 2 * CU)
            with sp.Fori(1, NCH) as n:
                merge(n, 1, m0 + n * MERGE_U, MERGE_U // 2)
            loads([(w_o, n * CW, KT) for n in range(NCH)], m0 + NCH * MERGE_U, MERGE_U // 2)

        @block.gpsimd
        def _(pool):
            pool.memset(half[:], -0.5).then_inc(pre["half"], 1)
            pool.wait_ge(pre["half"], 1)
            pool.memset(rel[32:33, :], 1.0).then_inc(pre["rel"], 1)
            pool.wait_ge(pre["rel"], 1)
            pool.wait_ge(pre["meanx"], 1)
            pool.tensor_tensor(rsx[:, 0:2], msx[:, 0:2], half[:, 0:2], ALU.pow).then_inc(pre["rootx"], 1)
            for i in range(2 * M_GROUPS):
                pool.wait_ge(means, i + 1)
                pool.tensor_tensor(rs[:, 0:4], ms[:, 0:4], half[:, 0:4], ALU.pow).then_inc(roots, 1)
                if i == 0:
                    pool.wait_ge(pre["meanm"], 1)
                    pool.wait_ge(pre["rootx"], 1)
                    pool.tensor_tensor(rsx[:, 2:4], msx[:, 2:4], half[:, 0:2], ALU.pow).then_inc(pre["rootm"], 1)
            with pool.Fori(2 * M_GROUPS, 2 * GROUPS) as i:
                pool.wait_ge(means, i + 1)
                pool.tensor_tensor(rs[:], ms[:], half[:], ALU.pow).then_inc(roots, 1)

        @block.scalar
        def _(act):
            def hi(u0, s, lc, before=BODY_U):
                ld = s // 2
                slot = ld % RING
                if fixed(u0, 0) and s == 0:
                    act.wait_ge(first_half_in, 16)
                else:
                    act.wait_ge(load_in[slot], 16 * lc[slot] + 16 * (ld // RING + 1))
                if s >= RING:
                    act.wait_ge(unit_used, u0 + s - RING + 1)
                elif not fixed(u0, 0):
                    act.wait_ge(unit_used, u0 + last_use(s, before) - before + 1)
                act.activation(whi[:, s % RING], raw[:, slot, UK * (s % 2):UK * (s % 2) + UK], ACT.Copy)\
                   .then_inc(hi_done, 1)

            act.dma_start(gx[:], norm_g.rearrange("l (p k) -> (l p) k", k=KT)).then_inc(gx_in, 16)
            act.dma_start(gm[:], mem_norm_g.rearrange("l (p k) -> (l p) k", k=KT)).then_inc(gx_in, 16)
            act.wait_ge(pre["half"], 1)
            act.activation(spare[:, 0:1], half[:, 0:1], ACT.Tanh)
            with nc.allow_non_contiguous_dma(reason="vectors of a few hundred words, once"):
                for i, (g, w) in enumerate(((q_norm_a, 1), (k_norm_a, 1), (q_norm_b, 1), (k_norm_b, 1),
                                            (q_norm_m, 2), (k_norm_m, 2))):
                    col = i if w == 1 else 4 + 2 * (i - 4)
                    act.dma_start(gains[:, col:col + w], g.rearrange("l (h p) -> p (l h)", p=P))\
                       .then_inc(small_in, 16)
            act.dma_start(rel[0:32, :], rel_bias).then_inc(small_in, 16)
            act.dma_start(oh[:], onehot).then_inc(small_in, 16)
            act.dma_start(bf[:], b_forget.to_broadcast([P, B_HEADS])).then_inc(small_in, 16)

            def tokens_hi(j):
                act.wait_ge(gx_in, 32)
                act.wait_ge(pre["xT"], j + 1)
                for i in range(2):
                    k = 2 * j + i
                    o = act.activation(hT[0][:, k], x_banks[j][:, i * S:(i + 1) * S], ACT.Copy, scale=gx[:, k:k + 1])
                o.then_inc(pre["x_hi"], 1)

            def beside_first(s):
                if s in (12, 13):
                    t = s - 12
                    if t:
                        act.wait_ge(pre["summ"], t)
                    act.activation(waste, mem_sb[:, t], ACT.Square, accum_out=ssx[:, 2 + t:3 + t])\
                       .then_inc(pre["summ"], 1)
                if s == 1:
                    with nc.allow_non_contiguous_dma(reason="eight columns, once"):
                        act.dma_start(wf[:], w_in_v[:, :, F0:F0 + B_HEADS]).then_inc(wf_in, 16)
                for r in range(2):
                    for j in range(4):
                        if s == 7 + 3 * r + j // 2:
                            act.wait_ge(pre["mTp"], 4 * r + j + 1)
                            for i in range(2):
                                k = 8 * r + 2 * j + i
                                o = act.activation(mT[0][:, k], side[j][:, i * S:(i + 1) * S], ACT.Copy,
                                                   scale=gm[:, k:k + 1])
                            o.then_inc(pre["mT_hi"], 1)
                if s == 9:
                    act.wait_ge(wf_in, 16)
                    act.activation(wf_hi, wf[:], ACT.Copy).then_inc(pre["wf_hi"], 1)
                if s == 17:
                    act.wait_ge(pre["vneg"], 1)
                    act.activation(ls[3][:], ls[2][:], ACT.Exp).then_inc(pre["e"], 1)
                if s == 15:
                    act.wait_ge(pre["dvec"], 1)
                    act.activation(dvec, side[2][0:A_HEADS, 0:SEG], ACT.Copy).then_inc(pre["dvec_sb"], 1)
                    act.wait_ge(pre["dvec_sb"], 1)
                    act.dma_start(rel_dram, dvec).then_inc(pre["dvec_out"], 16)
                if s == 19:
                    act.wait_ge(pre["u"], 1)
                    act.activation(ls[5][:], ls[4][:], ACT.Ln).then_inc(pre["ln"], 1)
                if s == 18:
                    act.wait_ge(pre["dvec_out"], 16)
                    for g in range(A_GROUPS):
                        for c0, n, d0 in ((0, 2 * P, 0), (P, P, 2 * P)):
                            src = bass.AP(rel_dram.tensor, g * 4 * SEG + P - 1 + c0, [[SEG, 4], [-1, P], [1, n]])
                            act.dma_start(bias_dram[g, :, :, d0:d0 + n].rearrange("p h c -> h p c"), src)\
                               .then_inc(bias_out, 16)
                if s == 25:
                    act.wait_ge(pre["crow_sb"], 1)
                    act.dma_start(crow_dram, cT).then_inc(pre["crow_out"], 16)
                if s == 27:
                    act.wait_ge(pre["crow_out"], 16)
                    for i in range(B_GROUPS):
                        rows = crow_dram[4 * i:4 * i + 4].rearrange("(o h) c -> o h c", o=1)
                        act.dma_start((bias, probs)[i][:, :, 0:S], rows.to_broadcast([P, 4, S]))\
                           .then_inc(pre["crow_in"], 16)
                if s == 31:
                    for i in range(B_GROUPS):
                        act.wait_ge(pre["fbias"], 2 * i + 2)
                        act.dma_start(bias_dram[A_GROUPS + i], (bias, probs)[i]).then_inc(bias_out, 16)

            def square(kind, w, c, norm, t):
                act.wait_ge(unit_used, CU * c + CU)
                if fixed(norm, 1):
                    act.wait_ge(pre["rootm"], 1)
                if fixed(norm, 0):
                    act.wait_ge(pre["rootx"], 1)
                else:
                    act.wait_ge(qkT_done, 2 * norm)
                r = t + (TT if kind == "m" and w else 0)
                act.activation(qn[:, t], acc[w][t][:], ACT.Square, scale=rsx[:, r:r + 1]).then_inc(squares, 1)

            def z_post(g, t):
                act.wait_ge(unit_used, BODY_U * g + BODY_U)
                if fixed(g, 0):
                    act.wait_ge(pre["halfx"], 1)
                else:
                    act.wait_ge(ozT_done, 2 * g)
                act.activation(silz[:, t], acc[1][t][:], ACT.Tanh, scale=hrx[:, t:t + 1]).then_inc(z_tanh, 1)

            def evac(kind, norm, which, bank, g):
                dst = (qT, kT)[which]
                act.wait_ge(qkT_done, 2 * norm + bank + 1)
                if not fixed(g, 0):
                    act.wait_ge(scores_done, 2 * g)
                else:
                    act.wait_ge(pre["mTp"], 8)
                act.wait_ge(pre["gains"], 1)
                ps = side[2 + bank]
                if kind == "m":
                    for i in range(2):
                        o = act.activation(dst[:, 2 * bank + i], ps[:, i * S:(i + 1) * S], ACT.Copy,
                                           scale=(gq, gk)[which][:, AB_GROUPS + i:AB_GROUPS + i + 1])
                else:
                    act.wait_ge(gains_set, g + 1 - M_GROUPS)
                    o = act.activation(dst[:, 2 * bank:2 * bank + 2], ps[:], ACT.Copy,
                                       scale=gcur[:, which:which + 1])
                o.then_inc(qkT_evac, 1)

            def exps(kind, a, step):
                act.wait_ge(logits_done, 2 * a + step + 1)
                if kind == "m":
                    if a > 0:
                        act.wait_ge(pv_done, 2 * a)
                    else:
                        act.wait_ge(bias_out, 16 * (2 * A_GROUPS + B_GROUPS))
                    for t in range(TT):
                        i = 2 * step + t
                        o = act.activation(probs_m[:, step, t], side[step][:, t * S:(t + 1) * S], ACT.Exp,
                                           bias=rmin[:, i:i + 1], scale=-1.0, accum_out=den[:, i:i + 1])
                else:
                    for h in (2 * step, 2 * step + 1):
                        for i, c0, n in ((2 * h, 0, 2 * P), (2 * h + 1, 2 * P, P)):
                            o = act.activation(probs[:, h, c0:c0 + n], probs[:, h, c0:c0 + n], ACT.Exp,
                                               bias=rmin[:, i:i + 1], scale=-1.0, accum_out=den[:, i:i + 1])
                o.then_inc(probs_done, 1)

            def split_oz(k0, a, bank):
                act.wait_ge(ozT_done, 2 * a + bank + 1)
                act.wait_ge(pre["fb"], 1)
                act.activation(ozT[0][:, bass.ds(k0 + 2 * bank, 2)], side[bank][:], ACT.Copy).then_inc(oz_hi, 1)

            def attention(kind, a, k0, s):
                if s in U_PROBS:
                    exps(kind, a, U_PROBS.index(s))
                if s in U_SPLIT:
                    split_oz(k0, a, U_SPLIT.index(s))

            def body(kind, g, b, lc, attn):
                u0 = g * BODY_U
                for s in range(BODY_U):
                    hi(u0, s, lc)
                    if attn is None:
                        for j in x_evac(s):
                            tokens_hi(j)
                    if attn is None:
                        beside_first(s)
                    else:
                        if s in U_Z:
                            z_post(attn[1], U_Z.index(s))
                        attention(*attn, s)
                    for w in range(2):
                        for t in range(TT):
                            if s == U_SQ[w] + t:
                                square(kind, w, 4 * g + w, 2 * g + w, t)
                            if s == U_EVAC[w] + t:
                                evac(kind, 2 * g + w, w, t, g)
                    if attn is not None and kind == "ab" and s == 11:
                        if not fixed(b, 0):
                            act.wait_ge(logits_done, 2 * g)
                            act.dma_start(bias, bias_dram[bass.ds(b, 1)].rearrange("g p h c -> (g p) h c"))\
                               .then_inc(bias_in, 16)
                        else:
                            act.wait_ge(bias_out, 16 * (2 * A_GROUPS + B_GROUPS))
                            act.dma_start(bias, bias_dram[0]).then_inc(bias_in, 16)

            per = 2 * CU // RING
            body("m", 0, 0, [0] * 4, None)
            body("m", 1, 1, [per] * 4, ("m", 0, OZ_M))
            body("ab", 2, 0, [2 * per] * 4, ("m", 1, OZ_M + 4))
            with act.Fori(1, AB_GROUPS) as b:
                body("ab", b + M_GROUPS, b, [(b + M_GROUPS) * per] * 4,
                     ("ab", b + M_GROUPS - 1, OZ_A + 4 * (b - 1)))

            m0 = GROUPS * BODY_U
            base = [GROUPS * per] * 4
            merge_l = [len(range(s, MERGE_U // 2, RING)) for s in range(RING)]

            def merged_split(n, bank):
                act.wait_ge(mergedT_done, 2 * n + bank + 1)
                act.wait_ge(unit_used, M_GROUPS * BODY_U)
                act.activation(mT[0][:, bass.ds(4 * n + 2 * bank, 2)], side[bank][:], ACT.Copy).then_inc(m_hi, 1)

            def merge(n, attn):
                lc = [base[s] + n * merge_l[s] for s in range(RING)]
                for s in range(MERGE_U):
                    hi(m0 + n * MERGE_U, s, lc, BODY_U if attn else MERGE_U)
                    if attn:
                        if s in U_Z:
                            z_post(attn[1], U_Z.index(s))
                        attention(*attn, s)
                    elif s in (8, 9):
                        merged_split(n - 1, s - 8)
                    if s == 7:
                        if attn:
                            act.wait_ge(logits_done, 2 * GROUPS)
                            for i, src in enumerate((2, 0, 1)):
                                act.dma_start(gate_b[:, i], b_gate[0, src:src + 1, 0:CW].to_broadcast([P, CW]))\
                                   .then_inc(gb_in, 16)
                        else:
                            act.wait_ge(chunk_taken, 2 * (4 * GROUPS + 6 * n))
                            for i, src in enumerate((2, 0, 1)):
                                act.dma_start(gate_b[:, i], b_gate[0, src:src + 1, bass.ds(n * CW, CW)]
                                              .to_broadcast([P, CW])).then_inc(gb_in, 16)
                    for i in range(3):
                        for t in range(TT):
                            if s == 8 * i + 11 + t:
                                act.wait_ge(chunk_taken, 2 * (4 * GROUPS + 6 * n) + 2 * i + t + 1)
                                act.activation(gates[i][:, t], gates[i][:, t], ACT.Tanh, scale=0.5)\
                                   .then_inc(gate_tanh, 1)

            merge(0, ("ab", GROUPS - 1, OZ_A + 4 * (AB_GROUPS - 1)))
            with act.Fori(1, NCH) as n:
                merge(n, None)

            lc = [base[s] + NCH * merge_l[s] for s in range(RING)]
            u0 = m0 + NCH * MERGE_U
            act.wait_ge(chunk_taken, 2 * (4 * GROUPS + 6 * NCH - 1))
            for n in range(NCH):
                act.dma_start(res[n], x_c[:, :, n * CW:(n + 1) * CW]).then_inc(res_in, 16)
            for s in range(NCH * CU):
                hi(u0, s, lc, MERGE_U)
                if s in (4, 5):
                    merged_split(NCH - 1, s - 4)
                if s >= CU and s % CU == 5:
                    n = s // CU - 1
                    act.wait_ge(chunk_taken, 2 * (4 * GROUPS + 6 * NCH + n + 1))
                    act.dma_start(out_v[:, :, n * CW:(n + 1) * CW], res[n]).then_inc(out_sem, 16)
            for t in range(TT):
                act.wait_ge(chunk_taken, 2 * (4 * GROUPS + 6 * NCH + NCH - 1) + t + 1)
                act.dma_start(out_v[:, t, (NCH - 1) * CW:], res[NCH - 1][:, t]).then_inc(out_sem, 16)
            act.wait_ge(out_sem, 16 * (NCH + 1))

        @block.vector
        def _(dve):
            def lo(u0, s):
                dve.wait_ge(hi_done, u0 + s + 1)
                dve.tensor_tensor(wlo[:, s % RING], raw[:, (s // 2) % RING, UK * (s % 2):UK * (s % 2) + UK],
                                  whi[:, s % RING].bitcast(F32), ALU.subtract).then_inc(lo_done, 1)

            def chain(name, n, ins):
                ins.then_inc(pre[name], 1)
                dve.wait_ge(pre[name], n)

            def token_squares(t, c0, n, col):
                dve.wait_ge(x_in[t], 16)
                if col:
                    dve.wait_ge(pre["sumx"], col)
                xr = raw[:, 2 + t].rearrange("p k c -> p (k c)")[:, c0:c0 + n]
                dve.tensor_tensor_reduce(out=waste[:, 0:n], in0=xr, in1=xr, scale=1.0, scalar=0.0, op0=ALU.mult,
                                         op1=ALU.add, accum_out=sqx[:, col:col + 1]).then_inc(pre["sumx"], 1)

            def tokens_lo(j):
                dve.wait_ge(gx_in, 32)
                dve.wait_ge(pre["x_hi"], j + 1)
                for i in range(2):
                    k = 2 * j + i
                    dve.scalar_tensor_tensor(hT[1][:, k], x_banks[j][:, i * S:(i + 1) * S], gx[:, k:k + 1],
                                             hT[0][:, k].bitcast(F32), ALU.mult, ALU.subtract)\
                       .then_inc(pre["x_lo"], 1)

            def norm_sums(g, norm, kind):
                heads, dim = (4, HD) if kind == "ab" else (2, MD)
                dve.wait_ge(squares, 2 * norm + 2)
                dve.reduce_sum(ss[:, 0:2 * heads], qn.rearrange("p t (h d) -> p (t h) d", d=dim), AX.X)\
                   .then_inc(sums, 1)
                dve.wait_ge(sums, norm + 1)
                dve.tensor_scalar(ms[:, 0:2 * heads], ss[:, 0:2 * heads], 1.0 / dim, EPS, ALU.mult, ALU.add)\
                   .then_inc(means, 1)

            def normalise(kind, norm, w, t):
                heads, dim = (4, HD) if kind == "ab" else (2, MD)
                dve.wait_ge(roots, norm + 1)
                if fixed(norm, 1):
                    dve.wait_ge(pre["rootm"], 1)
                r = rs[:, t * heads:(t + 1) * heads].rearrange("p (h o) -> p h o", o=1).to_broadcast([P, heads, dim])
                x = t + (TT if kind == "m" and w else 0)
                dve.scalar_tensor_tensor(qn[:, t].rearrange("p (h d) -> p h d", d=dim),
                                         acc[w][t][:].rearrange("p (h d) -> p h d", d=dim), rsx[:, x:x + 1], r,
                                         ALU.mult, ALU.mult).then_inc(chunk_taken, 1)

            def silu(g, t):
                dve.wait_ge(z_tanh, 2 * g + t + 1)
                dve.scalar_tensor_tensor(silz[:, t], silz[:, t], 1.0, acc[1][t][:], ALU.add, ALU.mult)\
                   .then_inc(chunk_taken, 1)

            def logits(kind, a, step):
                dve.wait_ge(scores_done, 2 * a + step + 1)
                if kind == "m":
                    dve.tensor_reduce(rmin[:, 2 * step:2 * step + 2], side[step][:].rearrange("p (t c) -> p t c", t=TT),
                                      AX.X, ALU.min).then_inc(logits_done, 1)
                    return
                dve.wait_ge(bias_in, 16 * (a - M_GROUPS) + 16)
                dve.wait_ge(pv_done, 2 * a)
                dve.memset(spare[:, step:step + 1], 0.0)
                for h in (2 * step, 2 * step + 1):
                    for i, c0, n in ((2 * h, 0, 2 * P), (2 * h + 1, 2 * P, P)):
                        o = dve.tensor_tensor_reduce(out=probs[:, h, c0:c0 + n], in0=side[h][:, c0:c0 + n],
                                                     in1=bias[:, h, c0:c0 + n], scale=1.0, scalar=3e38,
                                                     op0=ALU.add, op1=ALU.min, accum_out=rmin[:, i:i + 1])
                o.then_inc(logits_done, 1)

            def copy_probT(kind, a, step):
                dve.wait_ge(probT_done, 2 * a + step + 1)
                if kind == "m":
                    o = dve.tensor_copy(probs_m[:, step].rearrange("p t c -> p (t c)"), side[step][:])
                else:
                    for h in (2 * step, 2 * step + 1):
                        o = dve.tensor_copy(probs[:, h], side[h][:, 0:SEG])
                o.then_inc(probT_copied, 1)

            def half_inverse(kind, a):
                n = 8 if kind == "ab" else 4
                dve.wait_ge(probs_done, 2 * a + 2)
                dve.reciprocal(inv[:, 0:n], den[:, 0:n]).then_inc(inv_done, 1)
                dve.wait_ge(inv_done, a + 1)
                for t in range(TT):
                    first = t if kind == "m" else 1 - t
                    o = dve.tensor_scalar(rden[:, first:n:2], inv[:, first:n:2], hrx[:, t:t + 1], None, ALU.mult)
                o.then_inc(rden_done, 1)

            def gate_output(kind, a, step):
                dve.wait_ge(pv_done, 2 * a + step + 1)
                dve.wait_ge(rden_done, a + 1)
                dve.wait_ge(chunk_taken, 8 * a + 8)
                for j in range(2):
                    for t in range(TT):
                        if kind == "m":
                            if j:
                                continue
                            i, c0, n, ps = 2 * step + t, step * MD, MD, side[step][:, t * MD:(t + 1) * MD]
                        else:
                            h = 2 * step + j
                            i, c0, n = 2 * h + 1 - t, h * HD, HD
                            ps = side[step][:, j * S + t * P:j * S + (t + 1) * P]
                        o = dve.scalar_tensor_tensor(silz[:, t, c0:c0 + n], ps, rden[:, i:i + 1],
                                                     silz[:, t, c0:c0 + n], ALU.mult, ALU.mult)
                o.then_inc(oz_done, 1)

            def split_oz(k0, a, bank):
                dve.wait_ge(oz_hi, 2 * a + bank + 1)
                dve.tensor_tensor(ozT[1][:, bass.ds(k0 + 2 * bank, 2)],
                                  side[bank][:].rearrange("p (k s) -> p k s", k=2),
                                  ozT[0][:, bass.ds(k0 + 2 * bank, 2)].bitcast(F32), ALU.subtract).then_inc(oz_lo, 1)

            def attention(kind, a, k0, s):
                if s in U_LOGITS:
                    logits(kind, a, U_LOGITS.index(s))
                if s in U_COPY:
                    copy_probT(kind, a, U_COPY.index(s))
                if s == U_COPY[1] + 1:
                    half_inverse(kind, a)
                if s in U_OZ:
                    gate_output(kind, a, U_OZ.index(s))
                if s in U_SPLIT:
                    split_oz(k0, a, U_SPLIT.index(s))

            def forget_bias(i):
                tile = (bias, probs)[i]
                for h in range(4):
                    hh = 4 * i + h
                    o = dve.scalar_tensor_tensor(tile[:, h, 2 * P:], tile[:, h, 0:P], ccol[:, 0, hh:hh + 1],
                                                 causal[:, P:], ALU.subtract, ALU.add)
                o.then_inc(pre["fbias"], 1)
                dve.wait_ge(pre["fbias"], 2 * i + 1)
                for h in range(4):
                    hh = 4 * i + h
                    o = dve.scalar_tensor_tensor(tile[:, h, 0:2 * P], tile[:, h, 0:2 * P], ccol[:, 1, hh:hh + 1],
                                                 causal[:, 0:2 * P], ALU.subtract, ALU.add)
                o.then_inc(pre["fbias"], 1)

            def beside_first(s):
                if s == 6:
                    dve.wait_ge(pre["sumx"], 3)
                    dve.tensor_copy(ssx[:, 0:1], sqx[:, 0:1])
                    dve.tensor_tensor(ssx[:, 1:2], sqx[:, 1:2], sqx[:, 2:3], ALU.add).then_inc(pre["sumx"], 1)
                    dve.wait_ge(pre["sumx"], 4)
                    dve.tensor_scalar(msx[:, 0:2], ssx[:, 0:2], 1.0 / D, EPS, ALU.mult, ALU.add)\
                       .then_inc(pre["meanx"], 1)
                    dve.wait_ge(small_in, 16 * 9)
                    for i in range(AB_GROUPS):
                        c = 0 if i < A_GROUPS else 2
                        dve.tensor_scalar(gq[:, i:i + 1], gains[:, c:c + 1], -HD ** -0.5, None, ALU.mult)
                        dve.tensor_copy(gk[:, i:i + 1], gains[:, c + 1:c + 2])
                    dve.tensor_scalar(gq[:, AB_GROUPS:], gains[:, 4:6], -MD ** -0.5, None, ALU.mult)
                    dve.tensor_copy(gk[:, AB_GROUPS:], gains[:, 6:8]).then_inc(pre["gains"], 1)
                if s == 14:
                    dve.wait_ge(pre["summ"], TT)
                    dve.tensor_scalar(msx[:, 2:4], ssx[:, 2:4], 1.0 / D, EPS, ALU.mult, ALU.add)\
                       .then_inc(pre["meanm"], 1)
                if s == 8:
                    dve.wait_ge(pre["rootx"], 1)
                    dve.tensor_scalar(hrx[:], rsx[:, 0:2], 0.5, None, ALU.mult).then_inc(pre["halfx"], 1)
                if s == 9:
                    dve.wait_ge(pre["wf_hi"], 1)
                    dve.tensor_tensor(wf_lo, wf[:], wf_hi.bitcast(F32), ALU.subtract).then_inc(pre["wf_lo"], 1)
                for r in range(2):
                    for j in range(4):
                        if s == 7 + 3 * r + j // 2:
                            dve.wait_ge(pre["mT_hi"], 4 * r + j + 1)
                            for i in range(2):
                                k = 8 * r + 2 * j + i
                                o = dve.scalar_tensor_tensor(mT[1][:, k], side[j][:, i * S:(i + 1) * S],
                                                             gm[:, k:k + 1], mT[0][:, k].bitcast(F32),
                                                             ALU.mult, ALU.subtract)
                            o.then_inc(pre["mT_lo"], 1)
                if s == 14:
                    dve.wait_ge(pre["fbT"], 1)
                    dve.tensor_copy(fbT, side[0][0:B_HEADS, 0:S]).then_inc(pre["fbT_sb"], 1)
                if s == 16:
                    dve.wait_ge(pre["fb"], 1)
                    for t in range(TT):
                        o = dve.scalar_tensor_tensor(ls[0][:, t], side[1][:, t * B_HEADS:(t + 1) * B_HEADS],
                                                     rsx[:, t:t + 1], bf[:], ALU.mult, ALU.add)
                    chain("v0", 1, o)
                    chain("v1", 1, dve.tensor_scalar(ls[1][:], ls[0][:], -1.0, None, ALU.mult))
                    dve.tensor_tensor(ls[2][:], ls[0][:], ls[1][:], ALU.min).then_inc(pre["vneg"], 1)
                if s == 18:
                    dve.wait_ge(pre["e"], 1)
                    dve.tensor_scalar(ls[4][:], ls[3][:], 1.0, None, ALU.add).then_inc(pre["u"], 1)
                if s == 20:
                    dve.wait_ge(pre["ln"], 1)
                    chain("log1p", 1, dve.tensor_scalar(ls[1][:], ls[4][:], -1.0, None, ALU.add))
                    chain("log1p", 2, dve.tensor_tensor(ls[2][:], ls[3][:], ls[1][:], ALU.subtract))
                    chain("log1p", 3, dve.reciprocal(ls[6][:], ls[4][:]))
                    chain("log1p", 4, dve.tensor_tensor(ls[1][:], ls[2][:], ls[6][:], ALU.mult))
                    chain("log1p", 5, dve.tensor_tensor(ls[2][:], ls[1][:], ls[5][:], ALU.add))
                    chain("log1p", 6, dve.tensor_scalar(ls[6][:], ls[0][:], 0.0, None, ALU.min))
                    chain("log1p", 7, dve.tensor_tensor(ls[7][:], ls[6][:], ls[2][:], ALU.subtract))
                    dve.tensor_copy(ls[3][:], ls[7][:]).then_inc(pre["lf"], 1)
                if s == 23:
                    dve.wait_ge(pre["ccol"], 1)
                    dve.tensor_copy(ccol[:].rearrange("p t h -> p (t h)"), side[0][:, 0:TT * B_HEADS])\
                       .then_inc(pre["ccol_sb"], 1)
                    dve.tensor_copy(cT, side[1][0:B_HEADS, 0:S]).then_inc(pre["crow_sb"], 1)
                if s in (29, 30):
                    dve.wait_ge(pre["crow_in"], 16 * B_GROUPS)
                    dve.wait_ge(pre["ccol_sb"], 1)
                    dve.wait_ge(cst_in, 16)
                    forget_bias(s - 29)

            def body(kind, g, attn, b=None):
                u0 = g * BODY_U
                for s in range(BODY_U):
                    lo(u0, s)
                    if attn is None:
                        if s < 2:
                            token_squares(1, s * D // 2, D // 2, 1 + s)
                        for j in x_evac(s):
                            tokens_lo(j)
                    if s == 9 and kind == "ab":
                        dve.wait_ge(qkT_evac, 4 * g)
                        dve.wait_ge(pre["gains"], 1)
                        dve.tensor_copy(gcur[:, 0:1], gq[:, bass.ds(b, 1)])
                        dve.tensor_copy(gcur[:, 1:2], gk[:, bass.ds(b, 1)]).then_inc(gains_set, 1)
                    if attn is None:
                        beside_first(s)
                    else:
                        for t in range(TT):
                            if s == U_Z[t] + 1:
                                silu(attn[1], t)
                        attention(*attn, s)
                    for w in range(2):
                        if s == U_SQ[w] + 1:
                            norm_sums(g, 2 * g + w, kind)
                        for t in range(TT):
                            if s == U_NORM[w] + t:
                                normalise(kind, 2 * g + w, w, t)
                    if s in U_V:
                        t = U_V.index(s)
                        dve.wait_ge(unit_used, u0 + 3 * CU)
                        if attn is not None:
                            dve.wait_ge(pv_done, 2 * g)
                        else:
                            dve.wait_ge(pre["summ"], TT)
                        r = t + (TT if kind == "m" else 0)
                        dve.tensor_scalar(v_sb[:, t], acc[0][t][:], rsx[:, r:r + 1], None, ALU.mult)\
                           .then_inc(chunk_taken, 1)

            token_squares(0, 0, D, 0)
            body("m", 0, None)
            body("m", 1, ("m", 0, OZ_M))
            body("ab", 2, ("m", 1, OZ_M + 4), 0)
            with dve.Fori(1, AB_GROUPS) as b:
                body("ab", b + M_GROUPS, ("ab", b + M_GROUPS - 1, OZ_A + 4 * (b - 1)), b)

            m0 = GROUPS * BODY_U
            c0 = 4 * GROUPS

            def mix_last(n, t, c):
                dve.wait_ge(unit_used, m0 + n * MERGE_U + MERGE_U)
                dve.wait_ge(gate_tanh, 6 * n + 6)
                dve.wait_ge(mixed, 4 * n + 2)
                dve.scalar_tensor_tensor(product[:, t], gates[2][:, t], 1.0, acc[1][t][:], ALU.add, ALU.mult)\
                   .then_inc(chunk_taken, 1)
                dve.wait_ge(chunk_taken, 2 * c + t + 1)
                dve.tensor_tensor(merged[:, t], merged[:, t], product[:, t], ALU.add).then_inc(mixed, 1)

            def merged_split(n, bank):
                dve.wait_ge(m_hi, 2 * n + bank + 1)
                dve.tensor_tensor(mT[1][:, bass.ds(4 * n + 2 * bank, 2)],
                                  side[bank][:].rearrange("p (k s) -> p k s", k=2),
                                  mT[0][:, bass.ds(4 * n + 2 * bank, 2)].bitcast(F32), ALU.subtract).then_inc(m_lo, 1)

            def merge(n, attn):
                u0, c = m0 + n * MERGE_U, c0 + 6 * n
                for s in range(MERGE_U):
                    lo(u0, s)
                    if attn:
                        for t in range(TT):
                            if s == U_Z[t] + 1:
                                silu(attn[1], t)
                        attention(*attn, s)
                    else:
                        if s in (2, 3):
                            mix_last(n - 1, s - 2, c - 1)
                        if s in (8, 9):
                            merged_split(n - 1, s - 8)
                    for i in range(3):
                        for t in range(TT):
                            if s == 8 * i + 10 + t:
                                dve.wait_ge(unit_used, u0 + (i + 1) * CU)
                                dve.wait_ge(gb_in, 48 * n + 48)
                                if attn:
                                    dve.wait_ge(scores_done if i < 2 else pv_done, 2 * GROUPS)
                                dve.scalar_tensor_tensor(gates[i][:, t], acc[i % 2][t][:], rsx[:, t:t + 1],
                                                         gate_b[:, i], ALU.mult, ALU.add)\
                                   .then_inc(chunk_taken, 1)
                    if s in (30, 31):
                        t = s - 30
                        dve.wait_ge(unit_used, u0 + 3 * CU + PROJ_K[0] // UK)
                        dve.wait_ge(gate_tanh, 6 * n + 2)
                        if attn:
                            dve.wait_ge(ozT_done, 2 * GROUPS)
                        else:
                            dve.wait_ge(mergedT_done, 2 * n)
                        dve.scalar_tensor_tensor(merged[:, t], gates[0][:, t], 1.0, acc[1][t][:],
                                                 ALU.add, ALU.mult).then_inc(chunk_taken, 1)
                    if s in (36, 37):
                        t = s - 36
                        dve.wait_ge(unit_used, u0 + MERGE_U - PROJ_K[2] // UK)
                        dve.wait_ge(gate_tanh, 6 * n + 4)
                        dve.scalar_tensor_tensor(product[:, t], gates[1][:, t], 1.0, acc[0][t][:],
                                                 ALU.add, ALU.mult).then_inc(chunk_taken, 1)
                        dve.wait_ge(chunk_taken, 2 * c + 9 + t)
                        dve.tensor_tensor(merged[:, t], merged[:, t], product[:, t], ALU.add).then_inc(mixed, 1)

            merge(0, ("ab", GROUPS - 1, OZ_A + 4 * (AB_GROUPS - 1)))
            with dve.Fori(1, NCH) as n:
                merge(n, None)

            u0 = m0 + NCH * MERGE_U
            c = c0 + 6 * NCH

            def result(n, t):
                if n < NCH - 1:
                    dve.wait_ge(unit_used, u0 + (n + 1) * CU)
                else:
                    dve.wait_ge(tail_done, t + 1)
                dve.wait_ge(res_in, 16 * NCH)
                dve.scalar_tensor_tensor(res[n][:, t], acc[n % 2][t][:], 0.5, res[n][:, t], ALU.mult, ALU.add)\
                   .then_inc(chunk_taken, 1)

            for s in range(NCH * CU):
                lo(u0, s)
                if s < TT:
                    mix_last(NCH - 1, s, c - 1)
                if s in (4, 5):
                    merged_split(NCH - 1, s - 4)
                if s >= CU and s % CU in (2, 3):
                    result(s // CU - 1, s % CU - 2)
            for t in range(TT):
                result(NCH - 1, t)

        @block.tensor
        def _(pe):
            def passes(s, x_pair, k, j, t, banks, first, last):
                tok = slice(t * P, (t + 1) * P)
                hi, lo = x_pair[0][:, k + j, tok], x_pair[1][:, k + j, tok]
                pe.matmul(banks[t][:], hi, whi[:, s % RING, j], start=first and j == 0, stop=False)
                pe.matmul(banks[t][:], hi, wlo[:, s % RING, j], start=False, stop=False)
                return pe.matmul(banks[t][:], lo, whi[:, s % RING, j], start=False, stop=last and j == UK - 1)

            def unit(u0, s, x_pair, k, banks, first, last):
                pe.wait_ge(lo_done, u0 + s + 1)
                for j in range(UK):
                    if isinstance(u0, int) and u0 + s < CU:
                        pe.wait_ge(pre["x_lo"], k + j + 1)
                    for t in range(TT):
                        o = passes(s, x_pair, k, j, t, banks, first, last)
                o.then_inc(unit_used, 1)

            def chunk_free(c):
                pe.wait_ge(chunk_taken, 2 * c - 2)

            def transposes(banks, src, done):
                for blk in range(4):
                    for t in range(TT):
                        c0 = (blk % 2) * S + t * P
                        o = pe.transpose(banks[blk // 2][:, c0:c0 + P], src[:, t, blk * P:(blk + 1) * P], ident)
                    if blk % 2:
                        o.then_inc(done, 1)

            def scores(kind, a, step):
                pe.wait_ge(qkT_evac, 4 * a + 4)
                if fixed(a, 0):
                    pe.wait_ge(pre["crow_sb"], 1)
                else:
                    pe.wait_ge(oz_lo, 2 * a)
                if kind == "m":
                    for t in range(TT):
                        for i in range(2):
                            o = pe.matmul(side[step][:, t * S:(t + 1) * S], qT[:, 2 * step + i, t * P:(t + 1) * P],
                                          kT[:, 2 * step + i], start=i == 0, stop=i == 1)
                else:
                    for h in (2 * step, 2 * step + 1):
                        pe.matmul(side[h][:, 0:S], qT[:, h, P:S], kT[:, h], start=True, stop=True)
                        o = pe.matmul(side[h][:, S:SEG], qT[:, h, 0:P], kT[:, h, 0:P], start=True, stop=True)
                o.then_inc(scores_done, 1)

            def probT(kind, a, step):
                pe.wait_ge(probs_done, 2 * a + step + 1)
                if kind == "m":
                    for t in range(TT):
                        for k in range(TT):
                            c0 = (2 * t + k) * P
                            o = pe.transpose(side[step][:, c0:c0 + P], probs_m[:, step, t, k * P:(k + 1) * P], ident)
                else:
                    for h in (2 * step, 2 * step + 1):
                        for c0 in range(0, SEG, P):
                            o = pe.transpose(side[h][:, c0:c0 + P], probs[:, h, c0:c0 + P], ident)
                o.then_inc(probT_done, 1)

            def pv(kind, a, step):
                pe.wait_ge(probT_copied, 2 * a + step + 1)
                pe.wait_ge(chunk_taken, 8 * a + 6)
                bank = side[step]
                if kind == "m":
                    for t in range(TT):
                        for k in range(TT):
                            o = pe.matmul(bank[:, t * MD:(t + 1) * MD], probs_m[:, step, t, k * P:(k + 1) * P],
                                          v_sb[:, k, step * MD:(step + 1) * MD], start=k == 0, stop=k == 1)
                else:
                    for j in range(2):
                        h = 2 * step + j
                        cols = slice(h * HD, (h + 1) * HD)
                        pe.matmul(bank[:, j * S + P:(j + 1) * S], probs[:, h, 0:P], v_sb[:, 0, cols],
                                  start=True, stop=False)
                        pe.matmul(bank[:, j * S + P:(j + 1) * S], probs[:, h, P:2 * P], v_sb[:, 1, cols],
                                  start=False, stop=True)
                        o = pe.matmul(bank[:, j * S:j * S + P], probs[:, h, 2 * P:], v_sb[:, 0, cols],
                                      start=True, stop=True)
                o.then_inc(pv_done, 1)

            def attention(kind, a, k0, s):
                for step in range(2):
                    if s == S_SCORES[step]:
                        scores(kind, a, step)
                    if s == S_PROBT[step]:
                        probT(kind, a, step)
                if s == S_PV:
                    pv(kind, a, 0)
                    pv(kind, a, 1)
                if s == S_OZT:
                    pe.wait_ge(oz_done, 2 * a + 2)
                    transposes(side[0:2], silz, ozT_done)

            def tokens_T(t, js):
                xk = raw[:, 2 + t].rearrange("p q c -> p (q c)").rearrange("p (i k) -> p k i", k=KT)
                for j in js:
                    if j >= 6 and t == 0:
                        pe.wait_ge(pre["x_lo"], 2 * (j - 5))
                    for i in range(2):
                        c0 = i * S + t * P
                        o = pe.transpose(x_banks[j][:, c0:c0 + P], xk[:, 2 * j + i], ident)
                    if t == TT - 1:
                        o.then_inc(pre["xT"], 1)

            def keep_clock(n):
                for _ in range(n):
                    pe.transpose(acc[0][0][:, 0:P], ident, ident)

            pe.wait_ge(ident_in, 16)
            for t in range(TT):
                keep_clock((18, 16)[t])
                pe.wait_ge(x_in[t], 16)
                tokens_T(t, range(6))

            def beside_first(s):
                if s == 1:
                    for t in range(TT):
                        tokens_T(t, range(6, 8))
                if s in (6, 9):
                    r = (6, 9).index(s)
                    pe.wait_ge(mem_in, 16 * TT)
                    pe.wait_ge(*((pre["mT_lo"], 4) if r else (pre["x_lo"], KT)))
                    for k in range(8 * r, 8 * r + 8):
                        bank = side[(k % 8) // 2]
                        for t in range(TT):
                            mk = mem_sb[:, t].rearrange("p (i k) -> p k i", k=KT)
                            c0 = (k % 2) * S + t * P
                            o = pe.transpose(bank[:, c0:c0 + P], mk[:, k], ident)
                        if k % 2:
                            o.then_inc(pre["mTp"], 1)
                if s == 12:
                    pe.wait_ge(pre["mT_lo"], 8)
                    pe.wait_ge(pre["wf_lo"], 1)
                    for k in range(KT):
                        dst = side[0][0:B_HEADS, 0:S]
                        pe.matmul(dst, wf_hi[:, k], hT[0][:, k], start=k == 0, stop=False)
                        pe.matmul(dst, wf_hi[:, k], hT[1][:, k], start=False, stop=False)
                        o = pe.matmul(dst, wf_lo[:, k], hT[0][:, k], start=False, stop=k == KT - 1)
                    o.then_inc(pre["fbT"], 1)
                if s == 13:
                    pe.wait_ge(small_in, 16 * 9)
                    pe.wait_ge(pre["rel"], 1)
                    pe.matmul(side[2][0:A_HEADS, 0:SEG], rel[:], oh[:], start=True, stop=True)\
                      .then_inc(pre["dvec"], 1)
                if s == 15:
                    pe.wait_ge(pre["fbT_sb"], 1)
                    for t in range(TT):
                        o = pe.transpose(side[1][:, t * B_HEADS:(t + 1) * B_HEADS], fbT[:, t * P:(t + 1) * P],
                                         ident[0:B_HEADS, 0:B_HEADS])
                    o.then_inc(pre["fb"], 1)
                    pe.wait_ge(pre["dvec_sb"], 1)
                if s == 22:
                    pe.wait_ge(cst_in, 16)
                    pe.wait_ge(pre["lf"], 1)
                    pe.matmul(side[0][:, 0:B_HEADS], tri[:, 0:P], ls[7][:, 0], start=True, stop=True)
                    pe.matmul(side[0][:, B_HEADS:2 * B_HEADS], tri[:, P:S], ls[7][:, 0], start=True, stop=False)
                    pe.matmul(side[0][:, B_HEADS:2 * B_HEADS], tri[:, 0:P], ls[7][:, 1], start=False, stop=True)
                    pe.matmul(side[1][0:B_HEADS, 0:S], ls[7][:, 0], tri, start=True, stop=False)
                    pe.matmul(side[1][0:B_HEADS, P:S], ls[7][:, 1], tri[:, 0:P], start=False, stop=True)\
                      .then_inc(pre["ccol"], 1)

            def body(kind, g, attn):
                u0 = g * BODY_U
                for s in range(BODY_U):
                    w = s // CU
                    if attn is None:
                        beside_first(s)
                    else:
                        attention(*attn, s)
                    for i in range(2):
                        if s == (S_QT, S_KT)[i]:
                            pe.wait_ge(chunk_taken, 8 * g + 2 * i + 2)
                            if attn is not None:
                                pe.wait_ge(probT_copied, 2 * g)
                            if i or attn is not None:
                                pe.wait_ge(qkT_evac, 4 * g + 2 * i)
                            transposes(side[2:4], qn, qkT_done)
                    if s % CU == 0 and (attn is not None or w >= 2):
                        chunk_free(4 * g + w)
                    x_pair = hT
                    if kind == "m" and w in (1, 2):
                        x_pair = mT
                        if attn is None and s == CU:
                            pe.wait_ge(pre["mT_lo"], 4)
                        if attn is None and s == CU + CU // 2:
                            pe.wait_ge(pre["mT_lo"], 8)
                    unit(u0, s, x_pair, UK * (s % CU), acc[w % 2], s % CU == 0, s % CU == CU - 1)

            body("m", 0, None)
            body("m", 1, ("m", 0, OZ_M))
            body("ab", 2, ("m", 1, OZ_M + 4))
            with pe.Fori(1, AB_GROUPS) as b:
                body("ab", b + M_GROUPS, ("ab", b + M_GROUPS - 1, OZ_A + 4 * (b - 1)))

            m0 = GROUPS * BODY_U
            c0 = 4 * GROUPS

            def merge(n, attn):
                u0, c = m0 + n * MERGE_U, c0 + 6 * n
                s = 0
                chunks = [(hT, 0, KT)] * 3 + [(ozT, OZ_M, PROJ_K[0]), (ozT, OZ_A, PROJ_K[1]), (ozT, OZ_B, PROJ_K[2])]
                for w, (pair, k0, tiles) in enumerate(chunks):
                    chunk_free(c + w)
                    for k in range(0, tiles, UK):
                        if attn:
                            attention(*attn, s)
                            if w == 3 and k == 0:
                                pe.wait_ge(oz_lo, 2 * GROUPS)
                        elif s == 5:
                            pe.wait_ge(mixed, 4 * n)
                            transposes(side[0:2], merged, mergedT_done)
                        unit(u0, s, pair, k0 + k, acc[w % 2], k == 0, k == tiles - UK)
                        s += 1

            merge(0, ("ab", GROUPS - 1, OZ_A + 4 * (AB_GROUPS - 1)))
            with pe.Fori(1, NCH) as n:
                merge(n, None)

            u0, c = m0 + NCH * MERGE_U, c0 + 6 * NCH
            for s in range(NCH * CU):
                if s % CU == 0:
                    chunk_free(c + s // CU)
                if s == 4:
                    pe.wait_ge(mixed, 4 * NCH)
                    transposes(side[0:2], merged, mergedT_done)
                if s in (6, 7):
                    pe.wait_ge(m_lo, 2 * NCH - 7 + s)
                if s < NCH * CU - 1:
                    unit(u0, s, mT, UK * (s % CU), acc[(s // CU) % 2], s % CU == 0, s % CU == CU - 1)
                    continue
                pe.wait_ge(lo_done, u0 + s + 1)
                for t in range(TT):
                    for j in range(UK):
                        o = passes(s, mT, UK * (s % CU), j, t, acc[(s // CU) % 2], False, True)
                    o.then_inc(tail_done, 1)


_INS = ["x", "mem", "norm_g", "mem_norm_g", "w_in", "b_forget", "b_gate", "rel_bias", "q_norm_a", "k_norm_a",
        "q_norm_b", "k_norm_b", "q_norm_m", "k_norm_m", "w_mem_kv", "w_proj_a", "w_proj_b", "w_proj_m", "w_out"]


def shape_constants():
    p, c = np.arange(P)[:, None], np.arange(2 * P)[None, :]
    causal = np.where(c - P > p, MASKED, 0.0)
    consts = np.concatenate([np.eye(P), (c >= p) * 1.0, causal], axis=1).astype(np.float32)
    exact, buckets, far = 16, 32, 2048
    onehot = np.zeros((33, SEG), np.float32)
    for j in range(SEG):
        d = 2 * P - 1 - j
        inside = (0 <= d <= 128) + (d >= 0 and d % 4 == 0 and d <= 512) + (d >= 0 and d % 16 == 0 and d <= 2048)
        if not inside:
            onehot[32, j] = MASKED
            continue
        large = exact + int(np.float32(np.log(np.float32(max(d, 1)) / np.float32(exact))
                                       / np.float32(math.log(far / exact))) * np.float32(buckets - exact))
        onehot[d if d < exact else min(large, buckets - 1), j] = -1.0
        onehot[32, j] = -math.log(inside)
    return consts, onehot


def kernel(**inputs):
    import numpy as _np
    import concourse.bacc as _bacc
    from concourse import mybir as _mybir
    from concourse.bass_utils import run_bass_kernel_spmd as _run

    nc = _bacc.Bacc("TRN2", target_bir_lowering=False, num_devices=1, dynamic_dma_scratch_size=1024)
    arrays, args = {}, []
    consts, onehot = shape_constants()
    named = [(n, inputs[n]) for n in _INS] + [("consts", consts), ("onehot", onehot)]
    for name, value in named:
        a = _np.ascontiguousarray(value)
        arrays[f"in_{name}_dram"] = a
        args.append(nc.dram_tensor(f"in_{name}_dram", a.shape, _mybir.dt.from_np(a.dtype), kind="ExternalInput").ap())
    out = nc.dram_tensor("out_dram", (1, S, D), F32, kind="ExternalOutput").ap()
    hybrid_block(nc, *args, out)
    r = _run(nc, [arrays], core_ids=[0])
    return r.results[0]["out_dram"]
```
